# Optimizing a Trainium2 kernel written in Bass

```python
import jax, jax.numpy as jnp
from jax import lax
import numpy as np

D_MODEL = 1024
BATCH = 1
SEQ = 512
DEPTH = 2

SSM_HEADS = 32
SSM_HEAD_DIM = 64
D_INNER = SSM_HEADS * SSM_HEAD_DIM
SSM_GROUPS = 4
D_STATE = 128
CONV_WIDTH = 4
CHUNK = 128
CONV_DIM = D_INNER + 2 * SSM_GROUPS * D_STATE
ATT_HEADS = 8
ATT_KV_HEADS = 2
ATT_HEAD_DIM = 128
ATT_WIDTH = ATT_HEADS * ATT_HEAD_DIM
IDX_HEADS = 8
IDX_DIM = 64
TOPK_MAX = 256
Q_BLOCK = 128
PEER_HEADS = 8
N_KEYS = 128
N_EXPERTS = N_KEYS * N_KEYS
PEER_TOPK = 16
PEER_QDIM = 256
PEER_BLOCK = 64
PLE_DIM = 256
ROPE_THETA = 10000.0
EPS = 1e-6

SPLITS = [D_INNER, CONV_DIM, SSM_HEADS, ATT_WIDTH, ATT_KV_HEADS * ATT_HEAD_DIM,
          ATT_KV_HEADS * ATT_HEAD_DIM, IDX_HEADS * IDX_DIM, IDX_DIM, IDX_HEADS, 2 * D_MODEL]

kernel_name = "hybrid_ssd_dsa_peer_block"

def _split_points():
    pts, acc = [], 0
    for s in SPLITS[:-1]:
        acc += s
        pts.append(acc)
    return pts

def rms_norm(x, g):
    xf = x.astype(jnp.float32)
    y = xf * lax.rsqrt(jnp.mean(xf * xf, axis=-1, keepdims=True) + EPS)
    return (y * g.astype(jnp.float32)).astype(x.dtype)

def rope_tables(positions, dim):
    inv = 1.0 / (ROPE_THETA ** (jnp.arange(0, dim, 2, dtype=jnp.float32) / dim))
    ang = positions.astype(jnp.float32)[..., None] * inv
    return jnp.cos(ang), jnp.sin(ang)

def apply_rope(x, cos, sin):
    x1, x2 = jnp.split(x.astype(jnp.float32), 2, axis=-1)
    c = cos[:, :, None, :]
    s = sin[:, :, None, :]
    return jnp.concatenate([x1 * c - x2 * s, x1 * s + x2 * c], axis=-1).astype(x.dtype)

def causal_depthwise_conv(x, w, b):
    c = x.shape[-1]
    rhs = jnp.transpose(w)[:, None, :].astype(x.dtype)
    y = lax.conv_general_dilated(x, rhs, window_strides=(1,),
                                 padding=[(CONV_WIDTH - 1, 0)],
                                 dimension_numbers=('NWC', 'WIO', 'NWC'),
                                 feature_group_count=c)
    return y + b.astype(x.dtype)

def ssd_chunked(x, dt, A, B, C):
    b, l, h, p = x.shape
    g, n = B.shape[2], B.shape[3]
    r = h // g
    c = l // CHUNK
    X = (x * dt[..., None]).reshape(b, c, CHUNK, g, r, p)
    Adt = (dt * A).reshape(b, c, CHUNK, g, r)
    Bc = B.astype(jnp.float32).reshape(b, c, CHUNK, g, n)
    Cc = C.astype(jnp.float32).reshape(b, c, CHUNK, g, n)
    cs = jnp.moveaxis(jnp.cumsum(Adt, axis=2), 2, -1)
    causal = jnp.tril(jnp.ones((CHUNK, CHUNK), dtype=bool))
    Lmat = jnp.exp(jnp.where(causal, cs[..., :, None] - cs[..., None, :], -jnp.inf))
    CB = jnp.einsum('bclgn,bcsgn->bcgls', Cc, Bc)
    y_diag = jnp.einsum('bcgls,bcgrls,bcsgrp->bclgrp', CB, Lmat, X)
    decay = jnp.exp(cs[..., -1:] - cs)
    states = jnp.einsum('bclgn,bcgrl,bclgrp->bcgrpn', Bc, decay, X)
    chunk_decay = jnp.exp(cs[..., -1])

    def step(carry, inp):
        st, dec = inp
        return carry * dec[..., None, None] + st, carry

    init = jnp.zeros((b, g, r, p, n), dtype=X.dtype)
    _, prev = lax.scan(step, init, (jnp.moveaxis(states, 1, 0), jnp.moveaxis(chunk_decay, 1, 0)))
    prev = jnp.moveaxis(prev, 0, 1)
    y_off = jnp.einsum('bclgn,bcgrpn,bcgrl->bclgrp', Cc, prev, jnp.exp(cs))
    return (y_diag + y_off).reshape(b, l, h, p)

def ssm_branch(z, xbc, dt_raw, conv_w, conv_b, dt_bias, a_log, d_skip, norm_g):
    b, l, _ = z.shape
    xbc = jax.nn.silu(causal_depthwise_conv(xbc, conv_w, conv_b))
    xs, Bm, Cm = jnp.split(xbc, [D_INNER, D_INNER + SSM_GROUPS * D_STATE], axis=-1)
    xs = xs.reshape(b, l, SSM_HEADS, SSM_HEAD_DIM).astype(jnp.float32)
    Bm = Bm.reshape(b, l, SSM_GROUPS, D_STATE)
    Cm = Cm.reshape(b, l, SSM_GROUPS, D_STATE)
    dt = jax.nn.softplus(dt_raw.astype(jnp.float32) + dt_bias.astype(jnp.float32))
    A = -jnp.exp(a_log.astype(jnp.float32))
    y = ssd_chunked(xs, dt, A, Bm, Cm) + d_skip.astype(jnp.float32)[:, None] * xs
    y = y.reshape(b, l, D_INNER) * jax.nn.silu(z.astype(jnp.float32))
    yg = y.reshape(b, l, SSM_GROUPS, D_INNER // SSM_GROUPS)
    yg = yg * lax.rsqrt(jnp.mean(yg * yg, axis=-1, keepdims=True) + EPS)
    return (yg.reshape(b, l, D_INNER) * norm_g.astype(jnp.float32)).astype(z.dtype)

def dsa_branch(q, k, v, qi, ki, wi, cos_a, sin_a, cos_i, sin_i, qn_g, kn_g):
    b, l = q.shape[0], q.shape[1]
    q = apply_rope(rms_norm(q.reshape(b, l, ATT_HEADS, ATT_HEAD_DIM), qn_g), cos_a, sin_a)
    k = apply_rope(rms_norm(k.reshape(b, l, ATT_KV_HEADS, ATT_HEAD_DIM), kn_g), cos_a, sin_a)
    v = v.reshape(b, l, ATT_KV_HEADS, ATT_HEAD_DIM)
    qi = apply_rope(qi.reshape(b, l, IDX_HEADS, IDX_DIM), cos_i, sin_i)
    ki = apply_rope(ki.reshape(b, l, 1, IDX_DIM), cos_i, sin_i)[:, :, 0].astype(jnp.float32)
    topk = min(TOPK_MAX, l // 4)
    nblk = l // Q_BLOCK
    rep = ATT_HEADS // ATT_KV_HEADS
    key_pos = jnp.arange(l)

    def blockify(t):
        return jnp.moveaxis(t.reshape(b, nblk, Q_BLOCK, *t.shape[2:]), 1, 0)

    def one_block(args):
        blk, qb, qib, wib = args
        t_pos = blk * Q_BLOCK + jnp.arange(Q_BLOCK)
        s = jnp.einsum('bthd,bsd->bths', qib.astype(jnp.float32), ki) * (IDX_DIM ** -0.5)
        I = jnp.einsum('bth,bths->bts', wib.astype(jnp.float32), jax.nn.relu(s)) * (IDX_HEADS ** -0.5)
        causal = key_pos[None, :] <= t_pos[:, None]
        I = jnp.where(causal[None], I, -jnp.inf)
        _, idx = lax.top_k(I, topk)
        valid = idx <= t_pos[None, :, None]
        k_sel = jax.vmap(lambda kb, ib: kb[ib])(k, idx)
        v_sel = jax.vmap(lambda vb, ib: vb[ib])(v, idx)
        qg = qb.reshape(b, Q_BLOCK, ATT_KV_HEADS, rep, ATT_HEAD_DIM).astype(jnp.float32)
        sc = jnp.einsum('btgrd,btkgd->btgrk', qg, k_sel.astype(jnp.float32)) * (ATT_HEAD_DIM ** -0.5)
        sc = jnp.where(valid[:, :, None, None, :], sc, -jnp.inf)
        pr = jax.nn.softmax(sc, axis=-1)
        o = jnp.einsum('btgrk,btkgd->btgrd', pr, v_sel.astype(jnp.float32))
        return o.reshape(b, Q_BLOCK, ATT_WIDTH).astype(qb.dtype)

    out = lax.map(one_block, (jnp.arange(nblk), blockify(q), blockify(qi), blockify(wi)))
    return jnp.moveaxis(out, 0, 1).reshape(b, l, ATT_WIDTH)

def peer_ffn(xn, w_q, sub_keys, u_tab, v_tab):
    b, l, _ = xn.shape
    q = (xn @ w_q).reshape(b, l, PEER_HEADS, 2, PEER_QDIM // 2).astype(jnp.float32)
    s = jnp.einsum('blhpd,hpkd->blhpk', q, sub_keys.astype(jnp.float32))
    s1, i1 = lax.top_k(s[..., 0, :], PEER_TOPK)
    s2, i2 = lax.top_k(s[..., 1, :], PEER_TOPK)
    cand = (s1[..., :, None] + s2[..., None, :]).reshape(b, l, PEER_HEADS, PEER_TOPK * PEER_TOPK)
    cidx = (i1[..., :, None] * N_KEYS + i2[..., None, :]).reshape(b, l, PEER_HEADS, PEER_TOPK * PEER_TOPK)
    top_s, pos = lax.top_k(cand, PEER_TOPK)
    eidx = jnp.take_along_axis(cidx, pos, axis=-1)
    gate = jax.nn.softmax(top_s, axis=-1)
    nblk = l // PEER_BLOCK

    def blockify(t):
        return jnp.moveaxis(t.reshape(b, nblk, PEER_BLOCK, *t.shape[2:]), 1, 0)

    def one_block(args):
        xb, eb, gb = args
        u = u_tab[eb].astype(jnp.float32)
        a = jax.nn.gelu(jnp.einsum('btd,bthkd->bthk', xb.astype(jnp.float32), u), approximate=False) * gb
        return jnp.einsum('bthk,bthkd->btd', a, v_tab[eb].astype(jnp.float32)).astype(xb.dtype)

    out = lax.map(one_block, (blockify(xn), blockify(eidx), blockify(gate)))
    return jnp.moveaxis(out, 0, 1).reshape(b, l, -1)

def setup_inputs(seed: int = 0) -> dict:
    key = jax.random.key(seed)
    ks = jax.random.split(key, 24)
    f32 = jnp.float32
    n_in = sum(SPLITS)
    col_scale = jnp.concatenate([
        jnp.full((s,), 0.1 if i == 2 else 1.0, f32) for i, s in enumerate(SPLITS)]) * (D_MODEL ** -0.5)
    row_scale = jnp.concatenate([jnp.full((D_INNER,), D_INNER ** -0.5, f32),
                                 jnp.full((ATT_WIDTH,), ATT_WIDTH ** -0.5, f32)])
    dt0 = jnp.exp(jax.random.uniform(ks[6], (DEPTH, SSM_HEADS), f32,
                                     jnp.log(1e-3), jnp.log(1e-1)))
    x = jax.random.normal(ks[0], (BATCH, SEQ, D_MODEL), f32)
    p = jax.random.normal(ks[1], (DEPTH, BATCH, SEQ, PLE_DIM), f32)
    positions = (jax.random.randint(ks[2], (BATCH, 1), 0, 1024)
                 + jnp.arange(SEQ, dtype=jnp.int32)[None, :]).astype(jnp.int32)
    return {
        "x": x,
        "p": p,
        "positions": positions,
        "norm_mix": 1.0 + 0.02 * jax.random.normal(ks[3], (DEPTH, D_MODEL), f32),
        "w_in": jax.random.normal(ks[4], (DEPTH, D_MODEL, n_in), f32) * col_scale,
        "conv_w": 0.5 * jax.random.normal(ks[5], (DEPTH, CONV_DIM, CONV_WIDTH), f32),
        "conv_b": 0.02 * jax.random.normal(ks[7], (DEPTH, CONV_DIM), f32),
        "dt_bias": dt0 + jnp.log(-jnp.expm1(-dt0)),
        "a_log": jnp.log(jax.random.uniform(ks[8], (DEPTH, SSM_HEADS), f32, 1.0, 16.0)),
        "d_skip": 1.0 + 0.02 * jax.random.normal(ks[9], (DEPTH, SSM_HEADS), f32),
        "ssm_norm": 1.0 + 0.02 * jax.random.normal(ks[10], (DEPTH, D_INNER), f32),
        "q_norm": 1.0 + 0.02 * jax.random.normal(ks[11], (DEPTH, ATT_HEAD_DIM), f32),
        "k_norm": 1.0 + 0.02 * jax.random.normal(ks[12], (DEPTH, ATT_HEAD_DIM), f32),
        "w_branch": jax.random.normal(ks[13], (DEPTH, D_INNER + ATT_WIDTH, D_MODEL), f32) * row_scale[:, None],
        "w_out": jax.random.normal(ks[14], (DEPTH, D_MODEL, D_MODEL), f32) * (D_MODEL ** -0.5),
        "norm_ffn": 1.0 + 0.02 * jax.random.normal(ks[15], (DEPTH, D_MODEL), f32),
        "peer_wq": jax.random.normal(ks[16], (DEPTH, D_MODEL, PEER_HEADS * PEER_QDIM), f32) * (D_MODEL ** -0.5),
        "peer_keys": jax.random.normal(ks[17], (DEPTH, PEER_HEADS, 2, N_KEYS, PEER_QDIM // 2), f32) * ((PEER_QDIM // 2) ** -0.5),
        "peer_u": jax.random.normal(ks[18], (DEPTH, N_EXPERTS, D_MODEL), f32) * (D_MODEL ** -0.5),
        "peer_v": jax.random.normal(ks[19], (DEPTH, N_EXPERTS, D_MODEL), f32) * (PEER_HEADS ** -0.5),
        "norm_ple": 1.0 + 0.02 * jax.random.normal(ks[20], (DEPTH, D_MODEL), f32),
        "w_ple_gate": jax.random.normal(ks[21], (DEPTH, D_MODEL, D_MODEL), f32) * (D_MODEL ** -0.5),
        "w_ple_proj": jax.random.normal(ks[22], (DEPTH, PLE_DIM, D_MODEL), f32) * (PLE_DIM ** -0.5),
    }

def reference(x, p, positions, norm_mix, w_in, conv_w, conv_b, dt_bias, a_log, d_skip,
              ssm_norm, q_norm, k_norm, w_branch, w_out, norm_ffn, peer_wq, peer_keys,
              peer_u, peer_v, norm_ple, w_ple_gate, w_ple_proj):
    cos_a, sin_a = rope_tables(positions, ATT_HEAD_DIM)
    cos_i, sin_i = rope_tables(positions, IDX_DIM)
    pts = _split_points()
    for i in range(DEPTH):
        h = rms_norm(x, norm_mix[i])
        proj = h @ w_in[i]
        z, xbc, dt_raw, q, k, v, qi, ki, wi, gates = jnp.split(proj, pts, axis=-1)
        y_ssm = ssm_branch(z, xbc, dt_raw, conv_w[i], conv_b[i], dt_bias[i], a_log[i],
                           d_skip[i], ssm_norm[i])
        y_att = dsa_branch(q, k, v, qi, ki, wi, cos_a, sin_a, cos_i, sin_i,
                           q_norm[i], k_norm[i])
        g_ssm, g_att = jnp.split(jax.nn.sigmoid(gates.astype(jnp.float32)), 2, axis=-1)
        merged = (g_ssm * (y_ssm @ w_branch[i, :D_INNER]).astype(jnp.float32)
                  + g_att * (y_att @ w_branch[i, D_INNER:]).astype(jnp.float32))
        x = x + merged.astype(x.dtype) @ w_out[i]
        h = rms_norm(x, norm_ffn[i])
        x = x + peer_ffn(h, peer_wq[i], peer_keys[i], peer_u[i], peer_v[i])
        h = rms_norm(x, norm_ple[i])
        x = x + (jax.nn.sigmoid(h @ w_ple_gate[i]) * (p[i] @ w_ple_proj[i])).astype(x.dtype)
    return x


_drawn_inputs = setup_inputs


def setup_inputs(seed=0):
    import zlib

    import numpy as np

    out = dict(_drawn_inputs(seed))
    spreads = {}
    factors = {'q_norm': 4.39, 'k_norm': 4.701, 'norm_ple': 5.556}
    for name, (base, spread) in spreads.items():
        noise = np.random.default_rng([zlib.crc32(name.encode()), seed]).standard_normal(out[name].shape)
        drawn = base * np.exp(spread * noise) if base else spread * noise
        out[name] = __import__('jax').numpy.asarray(drawn.astype(out[name].dtype))
    for name, factor in factors.items():
        out[name] = (out[name] * factor).astype(out[name].dtype)
    return out
```

```python
from contextlib import ExitStack, contextmanager

import numpy as np

import concourse.bass as bass
from concourse import mybir

F32, F32R, BF16 = mybir.dt.float32, mybir.dt.float32r, mybir.dt.bfloat16
I32, U32 = mybir.dt.int32, mybir.dt.uint32
ACT = mybir.ActivationFunctionType
ALU = mybir.AluOpType
AX = mybir.AxisListType

P = 128
D_MODEL, SEQ, DEPTH = 1024, 512, 2
KT = D_MODEL // P
NT = SEQ // P
SSM_HEADS, HEAD_P, GROUPS = 32, 64, 4
D_INNER = SSM_HEADS * HEAD_P
D_STATE, CONV_W = 128, 4
R_HEADS = SSM_HEADS // GROUPS
GW = D_INNER // GROUPS
CONV_TILES = GW // P + 2
ATT_HEADS, KV_HEADS, ATT_D = 8, 2, 128
REP = ATT_HEADS // KV_HEADS
IDX_HEADS, IDX_D, TOPK = 8, 64, 128
PEER_HEADS, N_KEYS, PEER_K = 8, 128, 16
PLE = 256
EPS = 1e-6
BIG, GONE = -1e30, -3e38

UNIT = 1024
U_IDX, U_ATT, U_SSM, U_GATES, U_OUT, U_WQ = 5, 10, CONV_TILES + 8, 2 * KT, KT, 2 * PEER_HEADS
GATE_AT = (4, 4, 4, 4)
GATE_BUFS = 4
TO_TURN, TO_VALUES = 2, 3
NB = 4
BLOCKS = N_KEYS // NB
EARLY = N_KEYS // 2
U_PLE = 2 + KT
U_USED = U_IDX + KV_HEADS * U_ATT + GROUPS * U_SSM + U_GATES + U_OUT + U_WQ + 2 * N_KEYS + U_PLE
RAW_SLOTS, SLOTS = 2, 8
U_PAD = -U_USED % SLOTS
U_LAYER = U_USED + U_PAD

PAR, _at = {}, 0
for _n, _w in (("norm_mix", KT), ("norm_ffn", KT), ("norm_ple", KT), ("conv_w", GROUPS * CONV_TILES * CONV_W),
               ("conv_b", GROUPS * CONV_TILES), ("ssm_norm", D_INNER // P), ("dt_bias", SSM_HEADS),
               ("a_log", SSM_HEADS), ("d_skip", SSM_HEADS), ("q_norm", ATT_D), ("k_norm", ATT_D)):
    PAR[_n] = (_at, _at + _w)
    _at += _w
N_PAR, N_NORMS = _at, 3 * KT

CST, _at = {}, 0
ROPE = ATT_D // 2 + IDX_D // 2
for _n, _w in (("ident", P), ("ones", P), ("tri", P), ("causal", P), ("iota", P), ("inv", ROPE)):
    CST[_n] = (_at, _at + _w)
    _at += _w
N_CST = _at

MAGIC = 12582912.0
TWO_PI = [6.28125, 0.0019350051879882812, 3.0199159819e-07]
GRP = 32
N_GRP = SEQ // GRP
TB = 4
STEPS = 32
FILLS = STEPS * TB // GRP
ROWS = 4
U_LOOP = 8


class Tally:

    def __init__(self):
        self.n, self.terms = 0, None

    def next(self, k=1):
        self.n += k
        return self.now()

    def now(self):
        return self.n if self.terms is None else self.terms + self.n


class Channel:

    def __init__(self, sem, name, depth=1):
        self.ready, self.free, self.depth = sem(name + "_ready"), sem(name + "_free"), depth
        self.tallies = {}

    def _tally(self, who):
        if who not in self.tallies:
            self.tallies[who] = Tally()
        return self.tallies[who]

    def to_write(self, who="writer"):
        return self._tally(who).next()

    def to_read(self, who):
        return self._tally(who).next()

    def all_read(self, who="writer"):
        t = self._tally(who)
        return t.n + self.depth if t.terms is None else t.terms + (t.n + self.depth)

    def slot(self, who="writer"):
        return (self._tally(who).n - 1) % self.depth


@contextmanager
def repeat(engine, count, per):
    with engine.Fori(0, count) as i:
        kept = [(t, d, t.n, t.terms) for t, d in per]
        for t, d, _, terms in kept:
            t.terms = i * d if terms is None else terms + i * d
        yield i
        for t, d, n, terms in kept:
            assert t.n - n == d, (t.n - n, d)
            t.n, t.terms = n + count * d, terms


def build(nc, w, params, cst, pos, x, p_emb, keys, gates_dram, early_dram, mix_dram, out, depth):
    ctx = ExitStack()
    with ctx:
        names = set()

        def sb(name, shape, dt=F32, stack=ctx):
            assert name not in names, name
            names.add(name)
            return stack.enter_context(nc.sbuf_tensor(name, shape, dt))

        def sem(name):
            return ctx.enter_context(nc.semaphore(name))

        x_res = sb("x_res", [P, KT, SEQ])
        h_hi, h_lo = sb("h_hi", [P, KT, SEQ], F32R), sb("h_lo", [P, KT, SEQ], F32R)
        w_raw = sb("w_raw", [P, RAW_SLOTS, UNIT])
        w_hi, w_lo = sb("w_hi", [P, SLOTS, UNIT], F32R), sb("w_lo", [P, SLOTS, UNIT], F32R)
        zero = sb("zero", [P, 1])
        cs = sb("cst_sb", [P, N_CST])
        pn = sb("norms_sb", [P, depth, N_NORMS])
        pr = sb("par_sb", [P, N_PAR - N_NORMS])
        trig = sb("trig", [P, 2, NT, ROPE])
        ident, ones, tri, causal, iota, inv = (cs[:, a:b] for a, b in CST.values())
        sin_a, cos_a = trig[:, 0, :, 0:ATT_D // 2], trig[:, 1, :, 0:ATT_D // 2]
        sin_i, cos_i = trig[:, 0, :, ATT_D // 2:], trig[:, 1, :, ATT_D // 2:]

        phase = ExitStack()
        sq = sb("sq", [P, 2, SEQ], stack=phase)
        hf = sb("hf", [P, 2, SEQ], stack=phase)
        rs = sb("rs", [P, SEQ], stack=phase)
        ang = sb("ang", [P, 3, NT * ROPE], stack=phase)
        pos_i, pos_f = sb("pos_i", [P, NT], I32, stack=phase), sb("pos_f", [P, NT], stack=phase)
        phase.close()

        mix = ExitStack()
        y_att, y_ssm = sb("y_att", [P, KT, SEQ], stack=mix), sb("y_ssm", [P, KT, SEQ], stack=mix)
        dtb = {n: sb(n, [P, NT, SSM_HEADS], stack=mix) for n in ("dt", "adt", "cs_tok", "e_cs", "decay", "c_dec")}
        OFF = [P * j * (j + 1) // 2 for j in range(NT)]
        bias = sb("bias", [P, P * NT * (NT + 1) // 2], BF16, stack=mix)
        phase = ExitStack()
        small = sb("small", [P, NT, P], stack=phase)
        qi = sb("qi", [P, NT, 512], stack=phase)
        rt = sb("rt", [P, 4, 256], stack=phase)
        kid = sb("kid", [P, NT, P], stack=phase)
        qi_t, ki_t = sb("qi_t", [P, 4, SEQ], stack=phase), sb("ki_t", [P, SEQ], stack=phase)
        relu = sb("relu", [P, 2, SEQ], stack=phase)
        score = sb("score", [P, SEQ], stack=phase)
        top8 = sb("top8", [P, 8], stack=phase)
        wi = sb("wi", [P, NT, IDX_HEADS], stack=phase)
        gate_i = sb("gate_i", [P, 2, SEQ], stack=phase)
        dts = sb("dts", [P, 6, NT * SSM_HEADS], stack=phase)
        phase.close()
        phase = ExitStack()
        over = ExitStack()
        qk = sb("qk", [P, NT, REP + 1, ATT_D], stack=over)
        rt2 = sb("rt2", [P, 4, (REP + 1) * ATT_D // 2], stack=over)
        over.close()
        a_hi, a_lo = sb("a_hi", [P, 4, SEQ], F32R, stack=phase), sb("a_lo", [P, 4, SEQ], F32R, stack=phase)
        ssq = sb("ssq", [P, NT, REP + 1], stack=phase)
        v_sb = sb("v_sb", [P, NT, ATT_D], stack=phase)
        qk_t = sb("qk_t", [P, REP + 1, SEQ], stack=phase)
        mx, sm = sb("mx", [P, 4, 2], stack=phase), sb("sm", [P, 4, 2], stack=phase)
        p_t = sb("p_t", [P, 2, SEQ], stack=phase)
        over = ExitStack()
        sqq = sb("sqq", [P, REP + 1, ATT_D], stack=over)
        over.close()
        sc = sb("sc", [P, 4, SEQ], stack=phase)
        phase.close()
        phase = ExitStack()
        over = ExitStack()
        xdt = sb("xdt", [P, NT, GW], stack=over)
        b_t, c_t = sb("b_t", [P, SEQ], stack=over), sb("c_t", [P, SEQ], stack=over)
        b_tok = sb("b_tok", [P, NT, D_STATE], stack=over)
        cb = sb("cb", [P, NT, P], stack=over)
        over.close()
        s_hi, s_lo = sb("s_hi", [P, 4, SEQ], F32R, stack=phase), sb("s_lo", [P, 4, SEQ], F32R, stack=phase)
        over = ExitStack()
        yy, sz = sb("yy", [P, NT, GW], stack=over), sb("sz", [P, NT, GW], stack=over)
        over.close()
        gate_t = sb("gate_t", [P, GATE_BUFS, 2, SEQ], stack=phase)
        acc = sb("acc", [P, 2, SEQ], stack=phase)
        over = ExitStack()
        xs_t = sb("xs_t", [P, 2, SEQ], stack=over)
        over.close()
        dd = sb("dd", [P, 2, SEQ], stack=phase)
        prev = sb("prev", [P, GW], stack=phase)
        sss = sb("sss", [P, NT], stack=phase)
        phase.close()
        mix.close()

        peer = ExitStack()
        sel_t = sb("sel_t", [P, 3, SEQ], stack=peer)
        early = sb("early", [P, 2, SEQ], stack=peer)
        phase = ExitStack()
        pq_t = sb("pq_t", [P, 2 * PEER_HEADS, SEQ], stack=phase)
        key_sb = sb("key_sb", [P, 2 * PEER_HEADS, N_KEYS], stack=phase)
        ps = sb("ps", [P, 2 * PEER_HEADS, N_KEYS], stack=phase)
        cand = sb("cand", [P, PEER_HEADS, PEER_K * PEER_K], stack=phase)
        hot = cand[:].rearrange("p h (i j) -> p h i j", i=PEER_K)
        pv = sb("pv", [P, 2 * PEER_HEADS, PEER_K], stack=phase)
        pi = sb("pi", [P, 2 * PEER_HEADS, PEER_K], U32, stack=phase)
        pif = sb("pif", [P, 2 * PEER_HEADS, PEER_K], stack=phase)
        cv = sb("cv", [P, PEER_HEADS, PEER_K], stack=phase)
        ci = sb("ci", [P, 3, PEER_HEADS, PEER_K], U32, stack=phase)
        cif = sb("cif", [P, 2, PEER_HEADS, PEER_K], stack=phase)
        sel = sb("sel", [P, 3, PEER_HEADS, PEER_K], stack=phase)
        psum8 = sb("psum8", [P, PEER_HEADS], stack=phase)
        phase.close()
        phase = ExitStack()
        gbuf = sb("gbuf", [P, 2, N_KEYS, GRP], stack=phase)
        rows = sb("rows", [P, ROWS, 2, TB, N_KEYS], stack=phase)
        phase.close()
        phase = ExitStack()
        g_in = sb("g_in", [P, 2, N_GRP, NB, GRP], stack=phase)
        gel = sb("gel", [P, 2, SEQ], stack=phase)
        e_hi, e_lo = (sb(n, [P, 2, NB, SEQ], F32R, stack=phase) for n in ("e_hi", "e_lo"))
        over = ExitStack()
        back = sb("back", [P, 2, NB, SEQ], stack=over)
        over.close()
        pf = sb("pf", [P, 2, SEQ], stack=phase)
        p_hi, p_lo = sb("p_hi", [P, 2, SEQ], F32R, stack=phase), sb("p_lo", [P, 2, SEQ], F32R, stack=phase)
        phase.close()
        peer.close()

        phase = ExitStack()
        sb("ple_pad", [P, 5 * SEQ + 3 * NT * ROPE + 2 * NT], stack=phase)
        pp = sb("pp", [P, KT, SEQ], stack=phase)
        pg = sb("pg", [P, 2, SEQ], stack=phase)
        phase.close()

        bk = [ctx.enter_context(nc.psum_tensor(f"bank{b}", [P, 512], F32)) for b in range(8)]

        bank_free = [sem(f"bank{b}_free") for b in range(8)]
        to_act, to_dve = ([sem(f"bank{b}_{n}") for b in range(8)] for n in ("to_act", "to_dve"))
        n_fill, n_act, n_dve = ([Tally() for _ in range(8)] for _ in range(3))
        units = Channel(sem, "units", SLOTS)
        raw_in = [sem(f"raw_in{s}") for s in range(RAW_SLOTS)]
        cst_in, x_in, pos_in, norms_in, par_in = (sem(n) for n in ("cst_in", "x_in", "pos_in", "norms_in", "par_in"))
        zero_set, rope_arg, trig_done = sem("zero_set"), sem("rope_arg"), sem("trig_done")
        hid = Channel(sem, "hid")
        x_new = sem("x_new")
        squares = Channel(sem, "squares", 2)
        rs_root, hf_done, hh_done = sem("rs_root"), sem("hf_done"), sem("hh_done")
        qi_rope, qi_turned = sem("qi_rope"), sem("qi_turned")
        relus = Channel(sem, "relus", 2)
        dt_arg, dt_exp, adt_done, cs_exp = sem("dt_arg"), sem("dt_exp"), sem("adt_done"), sem("cs_exp")
        decay_arg, decay_done = sem("decay_arg"), sem("decay_done")
        qk_sq = Channel(sem, "qk_sq")
        qk_ss, qk_root, qk_rope, qk_turned = sem("qk_ss"), sem("qk_root"), sem("qk_rope"), sem("qk_turned")
        scores = Channel(sem, "scores", 4)
        probs, probs_n = sem("probs"), sem("probs_n")
        p_turn = Channel(sem, "p_turn", 2)
        a_chan = Channel(sem, "a_chan")
        a_high = sem("a_high")
        tap0, taps = sem("tap0"), sem("taps")
        conv_out = Channel(sem, "conv_out", 2)
        xdt_done, btok_done, sz_done = sem("xdt_done"), sem("btok_done"), sem("sz_done")
        diff, expd = sem("diff"), sem("expd")
        mt = Channel(sem, "mt", 2)
        xdec_done, state_done = sem("xdec_done"), sem("state_done")
        y_sq, y_root, y_norm = sem("y_sq"), sem("y_root"), sem("y_norm")
        s_chan, s_high = Channel(sem, "s_chan"), sem("s_high")
        gate_s = Channel(sem, "gate_s", GATE_BUFS)
        gate_out = [sem(f"gate_out{s}") for s in range(2)]
        gate_landed = [sem(f"gate_landed{s}") for s in range(GATE_BUFS)]
        key_in, pq_done, ps_done = sem("key_in"), sem("pq_done"), Channel(sem, "ps_done")
        gate_arg, gate_exp = sem("gate_arg"), sem("gate_exp")
        sel_done, sel_turned = Channel(sem, "sel_done"), sem("sel_turned")
        onehot = Channel(sem, "onehot", ROWS)
        g_out = [sem("g_out0"), sem("g_out1")]
        early_out = [sem("early_out0"), sem("early_out1")]
        g_load = Channel(sem, "g_load", 2)
        g_landed = [sem("g_landed0"), sem("g_landed1")]
        back_landed = [sem("back_landed0"), sem("back_landed1")]
        gelus, e_prod, e_high = Channel(sem, "gelus", 2), sem("e_prod"), sem("e_high")
        e_chan = Channel(sem, "e_chan", 2 * NB)
        p_in, p_high, p_split, pp_done = sem("p_in"), sem("p_high"), sem("p_split"), sem("pp_done")
        pg_chan = Channel(sem, "pg_chan", 2)
        out_done = sem("out_done")

        def ple_bank(m):
            return (4, 1, 2, 3, 5, 6, 7, 4)[m]

        Z_BANKS = (7, 6, 7, 4)

        GATE_BANKS = (0, 4, 1, 5)

        block = ctx.enter_context(nc.Block())

        @block.sync
        def _(sp):
            sp.dma_start(cs[:], cst).then_inc(cst_in, 16)
            sp.dma_start(pos_i[:], pos).then_inc(pos_in, 16)
            sp.dma_start(x_res[:], x).then_inc(x_in, 16)
            sp.dma_start(pn[:], params[:, :, 0:N_NORMS]).then_inc(norms_in, 16)
            sp.dma_start(pr[:], params[:, 0, N_NORMS:]).then_inc(par_in, 16)
            for s in range(RAW_SLOTS):
                sp.dma_start(w_raw[:, s], w[s]).then_inc(raw_in[s], 16)
            with sp.Fori(0, depth * U_LAYER // RAW_SLOTS - 1) as i:
                for s in range(RAW_SLOTS):
                    sp.wait_ge(units.ready, i * RAW_SLOTS + (s + 1))
                    sp.dma_start(w_raw[:, s], w[i * RAW_SLOTS + (s + RAW_SLOTS)]).then_inc(raw_in[s], 16)
            sp.wait_ge(x_new, 3 * KT * depth)
            sp.dma_start(out, x_res[:]).then_inc(out_done, 16)
            sp.wait_ge(out_done, 16)
            for s in range(2):
                sp.wait_ge(g_out[s], 16 * (depth * N_GRP // 2 + 1))
                sp.wait_ge(early_out[s], 16 * (depth * EARLY // 2 + 1))
                sp.wait_ge(gate_out[s], 16 * (depth * KT + 1))

        @block.gpsimd
        def _(pool):
            pool.memset(zero[:], 0.0).then_inc(zero_set, 1)
            pool.wait_ge(zero_set, 1)
            zeros = zero[:].broadcast_to([P, UNIT])

            def split(n):
                units.to_write()
                s = units.slot()
                pool.wait_ge(raw_in[n % RAW_SLOTS], raw_tally[n % RAW_SLOTS].next(16))
                pool.wait_ge(units.free, units._tally("writer").now())
                pool.tensor_tensor(w_hi[:, s], w_raw[:, n % RAW_SLOTS], zeros, ALU.add)
                pool.drain()
                pool.tensor_tensor(w_lo[:, s], w_raw[:, n % RAW_SLOTS], w_hi[:, s].bitcast(F32),
                                   ALU.subtract).then_inc(units.ready, 1)

            raw_tally = [Tally() for _ in range(RAW_SLOTS)]
            tw = units._tally("writer")
            head = U_USED - U_PLE - 2 * N_KEYS
            odd = head % SLOTS
            for L in range(depth):
                with repeat(pool, head // SLOTS, [(tw, SLOTS)] + [(t, SLOTS // RAW_SLOTS * 16) for t in raw_tally]):
                    for n in range(SLOTS):
                        split(n)
                for n in range(odd):
                    split(n)
                rest = U_LAYER - head
                first = -odd % SLOTS
                for n in range(first):
                    split(odd + n)
                with repeat(pool, (rest - first) // SLOTS,
                            [(tw, SLOTS)] + [(t, SLOTS // RAW_SLOTS * 16) for t in raw_tally]):
                    for n in range(SLOTS):
                        split(n)

        @block.tensor
        def _(pe):
            for b in range(8):
                pe.sem_inc(bank_free[b], 1)
            for c in [units, hid, squares, relus, qk_sq, scores, p_turn, a_chan, conv_out, mt, s_chan,
                      gate_s, ps_done, sel_done, onehot, g_load, gelus, e_chan, pg_chan]:
                pe.sem_inc(c.free, c.depth)
            for s in g_out + early_out + gate_out:
                pe.sem_inc(s, 16)
            W, A = (w_hi, w_lo), (h_hi, h_lo)
            THREE = ((0, 0), (0, 1), (1, 0))

            used, due = [0], [0]

            def take(n=1):
                due[0], used[0] = due[0] + used[0], n
                slots = []
                for _ in range(n):
                    pe.wait_ge(units.ready, units.to_read("pe"))
                    slots.append(units.slot("pe"))
                return slots[0] if n == 1 else slots

            def hand_back(mm):
                if due[0]:
                    mm.then_inc(units.free, due[0])
                due[0] = 0

            def settle():
                pe.drain().then_inc(units.free, due[0] + used[0])
                due[0] = used[0] = 0

            def fill(b):
                pe.wait_ge(bank_free[b], n_fill[b].next())
                return bk[b]

            h_seen = [KT]

            def h_ready(k):
                if k >= h_seen[0]:
                    pe.wait_ge(hid.ready, hid.to_read("pe"))
                    h_seen[0] = k + 1

            def rows_of(o, s, at, n, k, j, first, last):
                h_ready(k)
                for q, (a, b) in enumerate(THREE):
                    mm = pe.matmul(o, A[b][:, k, j * P:(j + 1) * P], W[a][:, s, at:at + n],
                                   start=first and q == 0, stop=last and q == 2)
                    if q == 0:
                        hand_back(mm)
                return mm

            def cols_of(o, s, at, act, first, last):
                for q, (a, b) in enumerate(THREE):
                    mm = pe.matmul(o, W[a][:, s, at:at + P], act[b], start=first and q == 0, stop=last and q == 2)
                    if q == 0:
                        hand_back(mm)
                return mm

            def token_rows(b0, n_units, per, n, reader):
                for u in range(n_units):
                    s = take()
                    for j in range(NT):
                        o = fill(b0 + j) if u == 0 else bk[b0 + j]
                        for kk in range(per):
                            k = per * u + kk
                            mm = rows_of(o[:, 0:n], s, kk * n, n, k, j, k == 0, k == KT - 1)
                        if u == n_units - 1:
                            mm.then_inc(reader[b0 + j], 1)

            def channel_tile(b, reader):
                s = take()
                o = fill(b)
                for k in range(KT):
                    h_ready(k)
                    mm = cols_of(o[:], s, k * P, (A[0][:, k], A[1][:, k]), k == 0, k == KT - 1)
                mm.then_inc(reader[b], 1)

            def channel_tiles(n_tiles, reader):
                h_seen[0] = 0
                slots = take(4)
                banks = [fill(b) for b in range(4)]
                for k in range(KT):
                    h_ready(k)
                    for b in range(4):
                        mm = cols_of(banks[b][:], slots[b], k * P, (A[0][:, k], A[1][:, k]), k == 0, k == KT - 1)
                        if k == KT - 1:
                            mm.then_inc(reader[b], 1)
                for n in range(4, n_tiles):
                    channel_tile(n % 4, reader)

            def branch(chan, a_parts):
                pe.wait_ge(chan.ready, chan.to_read("pe"))
                for u in range(4):
                    s = take()
                    for mmi in range(2):
                        b = 6 + mmi
                        o = fill(b)
                        for k in range(4):
                            mm = cols_of(o[:], s, (mmi * 4 + k) * P, (a_parts[0][:, k], a_parts[1][:, k]), k == 0, k == 3)
                        mm.then_inc(to_dve[b], 1)

            def norm():
                o = fill(0)
                for m in range(KT):
                    pe.wait_ge(squares.ready, squares.to_read("pe"))
                    mm = pe.matmul(o[:], ones, sq[:, m % 2], start=m == 0, stop=m == KT - 1)
                    mm.then_inc(squares.free, 1)
                pe.drain().then_inc(to_act[0], 1)

            def turn(b, tiles, reader):
                o = fill(b)
                for i, t in enumerate(tiles):
                    mm = pe.transpose(o[:, i * P:(i + 1) * P], t, ident)
                mm.then_inc(reader[b], 1)

            t_qrope, t_qturn, t_adt, t_qkrope, t_qkturn, t_pn = (Tally() for _ in range(6))
            t_btok, t_xdt, t_xdec, t_state, t_ynorm, t_pq = (Tally() for _ in range(6))
            pe.wait_ge(cst_in, 16)
            for L in range(depth):
                norm()
                h_seen[0] = 0
                token_rows(0, 4, 2, 512, to_dve)
                s, o = take(), fill(4)
                for j in range(NT):
                    for k in range(KT):
                        mm = rows_of(o[:, j * P:(j + 1) * P], s, k * P, P, k, j, k == 0, k == KT - 1)
                mm.then_inc(to_dve[4], 1)
                for n in range(GATE_AT[0]):
                    channel_tile(5 + n % 2, to_act)
                pe.wait_ge(adt_done, t_adt.next())
                o = fill(7)
                adt2 = dtb["adt"][:].rearrange("p c h -> p (c h)")
                pe.matmul(o[:, 0:P], tri, adt2, start=True, stop=True)
                pe.matmul(o[:, P:2 * P], ones, adt2, start=True, stop=True).then_inc(to_act[7], 1)
                pe.wait_ge(qi_rope, t_qrope.next(NT + 1))
                for n in range(4):
                    turn(5 + n % 2, [qi[:, j, n * P:(n + 1) * P] for j in range(NT)], to_act)
                turn(5, [kid[:, j] for j in range(NT)], to_act)
                pe.wait_ge(qi_turned, t_qturn.next(5))
                for j in range(1, NT):
                    for h in range(IDX_HEADS):
                        b, half = h % 4, 64 * (h % 2)
                        o = fill(b)
                        pe.matmul(o[:, 0:(j + 1) * P], qi_t[half:half + 64, h // 2, j * P:(j + 1) * P],
                                  ki_t[half:half + 64, 0:(j + 1) * P], start=True, stop=True).then_inc(to_act[b], 1)
                        if j > 1 and h == 3:
                            for n in range(GATE_AT[1] // 2):
                                channel_tile(5 + n % 2, to_act)
                for g in range(KV_HEADS):
                    token_rows(0, 4, 2, 512, to_act)
                    token_rows(4, 2, 4, 256, to_act)
                    for n in range(GATE_AT[2 + g]):
                        channel_tile(GATE_BANKS[n], to_act)
                    pe.wait_ge(qk_rope, t_qkrope.next())
                    for n in range(REP + 1):
                        turn(n % 4, [qk[:, j, n] for j in range(NT)], to_act)
                    pe.wait_ge(qk_turned, t_qkturn.next(REP + 1))
                    steps = [(h, j) for h in range(REP) for j in range(NT)]
                    for s in range(len(steps) + TO_VALUES):
                        if s < len(steps):
                            h, j = steps[s]
                            o = fill(s % 2)
                            pe.matmul(o[:, 0:(j + 1) * P], qk_t[:, h, j * P:(j + 1) * P], qk_t[:, REP, 0:(j + 1) * P],
                                      start=True, stop=True).then_inc(to_dve[s % 2], 1)
                        if 0 <= s - TO_TURN < len(steps):
                            h, j = steps[s - TO_TURN]
                            pe.wait_ge(probs_n, t_pn.next())
                            b = 2 + s % 2
                            o = fill(b)
                            for i in range(j + 1):
                                mm = pe.transpose(o[:, i * P:(i + 1) * P], sc[:, (s - TO_TURN) % 4, i * P:(i + 1) * P], ident)
                            mm.then_inc(to_act[b], 1)
                        if 0 <= s - TO_VALUES < len(steps):
                            h, j = steps[s - TO_VALUES]
                            pe.wait_ge(p_turn.ready, p_turn.to_read("pe"))
                            o = fill(4 + h % 2) if j == 0 else bk[4 + h % 2]
                            for i in range(j + 1):
                                mm = pe.matmul(o[:, j * P:(j + 1) * P], v_sb[:, i], p_t[:, (s - TO_VALUES) % 2, i * P:(i + 1) * P],
                                               start=i == 0, stop=i == j)
                            mm.then_inc(p_turn.free, 1)
                            if j == NT - 1:
                                pe.drain().then_inc(to_act[4 + h % 2], 1)
                    branch(a_chan, (a_hi, a_lo))
                def z_quarters(first, n):
                    for i in range(first, first + n):
                        j, u = i // 4, i % 4
                        b = Z_BANKS[j]
                        o = fill(b) if u == 0 else bk[b]
                        for k in (2 * u, 2 * u + 1):
                            mm = rows_of(o[:], z_slots[u], k % 2 * 512, 512, k, j, k == 0, k == KT - 1)
                    if u == 3:
                        mm.then_inc(to_act[b], 1)

                for g in range(GROUPS):
                    for n in range(CONV_TILES + 2):
                        if n < CONV_TILES:
                            if n > 0 or g == 0:
                                channel_tile(n % 4, to_act)
                        else:
                            if n == CONV_TILES:
                                z_slots = take(4)
                            z_quarters(2 * (n - CONV_TILES), 2)
                        if n >= 2 and n != 3:
                            m = n - 2
                            pe.wait_ge(conv_out.ready, conv_out.to_read("pe"))
                            src = b_t if m == 0 else xs_t[:, m % 2]
                            turn(4 + m % 2, [src[:, c * P:(c + 1) * P] for c in range(NT)], to_act if m == 0 else to_dve)
                            pe.drain().then_inc(conv_out.free, 1)
                        elif n == 3:
                            pe.wait_ge(conv_out.ready, conv_out.to_read("pe"))
                            o = fill(6)
                            for c in range(NT):
                                mm = pe.matmul(o[:, c * P:(c + 1) * P], b_t[:, c * P:(c + 1) * P],
                                               c_t[:, c * P:(c + 1) * P], start=True, stop=True)
                            mm.then_inc(to_dve[6], 1)
                            pe.drain().then_inc(conv_out.free, 1)
                    pe.wait_ge(xdt_done, t_xdt.next(GW // P))
                    for r in range(R_HEADS + 2):
                        if r < R_HEADS:
                            o = fill(4 + r % 2)
                            for c in range(NT):
                                mm = pe.matmul(o[:, c * P:(c + 1) * P],
                                               dtb["adt"][:, c, g * R_HEADS + r:g * R_HEADS + r + 1].broadcast_to([P, P]),
                                               tri, start=True, stop=True)
                            mm.then_inc(to_dve[4 + r % 2], 1)
                        if 1 <= r <= 8:
                            z_quarters(3 + r, 1)
                        if r >= 2:
                            q = r - 2
                            pe.wait_ge(mt.ready, mt.to_read("pe"))
                            for c in range(NT):
                                o = fill(c) if q == 0 else bk[c]
                                mm = pe.matmul(o[:, q * HEAD_P:(q + 1) * HEAD_P], dd[:, q % 2, c * P:(c + 1) * P],
                                               xdt[:, c, q * HEAD_P:(q + 1) * HEAD_P], start=True, stop=True)
                                if q == R_HEADS - 1:
                                    mm.then_inc(to_dve[c], 1)
                            (pe.drain() if q == R_HEADS - 1 else mm).then_inc(mt.free, 1)
                    pe.wait_ge(btok_done, t_btok.next())
                    for c in range(NT - 1):
                        pe.wait_ge(xdec_done, t_xdec.next())
                        o = fill(6)
                        pe.matmul(o[:], b_tok[:, c], acc[:, 0], start=True, stop=True).then_inc(to_dve[6], 1)
                        if c < 2:
                            z_quarters(12 + 2 * c, 2)
                        pe.wait_ge(state_done, t_state.next())
                        o = fill(7)
                        pe.matmul(o[:], c_t[:, (c + 1) * P:(c + 2) * P], prev[:], start=True, stop=True)\
                          .then_inc(to_dve[7], 1)
                    if g < GROUPS - 1:
                        channel_tile(0, to_act)
                    else:
                        pe.drain().then_inc(hid.free, 1)
                    pe.wait_ge(y_norm, t_ynorm.next())
                    for i in range(4):
                        turn(4 + i % 2, [yy[:, c, i * P:(i + 1) * P] for c in range(NT)], to_act)
                    branch(s_chan, (s_hi, s_lo))
                channel_tiles(KT, to_dve)
                pe.drain().then_inc(hid.free, 1)
                norm()
                channel_tiles(2 * PEER_HEADS, to_act)
                pe.wait_ge(pq_done, t_pq.next(2 * PEER_HEADS))
                pe.wait_ge(key_in, 16 * (L + 1))

                def key_scores(j):
                    for q in range(4):
                        o = fill(q)
                        for i in range(4):
                            n = 4 * q + i
                            mm = pe.matmul(o[:, i * P:(i + 1) * P], pq_t[:, n, j * P:(j + 1) * P], key_sb[:, n],
                                           start=True, stop=True)
                        mm.then_inc(to_act[q], 1)

                key_scores(0)
                for j in range(NT):
                    for u in range(EARLY // 2 // NT):
                        if u == 4 and j + 1 < NT:
                            key_scores(j + 1)
                        channel_tile(4 + u % 2, to_act)
                    pe.wait_ge(sel_done.ready, sel_done.to_read("pe"))
                    turn(6, [sel[:, i].rearrange("p h k -> p (h k)") for i in range(3)], to_act)
                    pe.drain().then_inc(sel_done.free, 1)
                settle()
                with repeat(pe, SEQ // TB // STEPS, [(onehot._tally("pe"), STEPS), (units._tally("pe"), U_LOOP)]
                            + [(n_fill[b], STEPS // 4) for b in range(4)]
                            + [(n_fill[b], U_LOOP // 2) for b in (4, 5)]):
                    for n in range(STEPS):
                        b = n % 4
                        pe.wait_ge(onehot.ready, onehot.to_read("pe"))
                        o = fill(b)
                        for t in range(TB):
                            mm = pe.matmul(o[:, t * P:(t + 1) * P], rows[:, n % ROWS, 0, t], rows[:, n % ROWS, 1, t],
                                           start=True, stop=True)
                            if t == 0 and n > 0:
                                mm.then_inc(onehot.free, 1)
                        mm.then_inc(to_act[b], 1)
                        if n % 2 == 1:
                            if n % 4 == 1:
                                s, o = take(), fill(4 + n // 4 % 2)
                            half = range(KT // 2) if n % 4 == 1 else range(KT // 2, KT)
                            if n % 4 == 3:
                                o = bk[4 + n // 4 % 2]
                            for k in half:
                                mm = cols_of(o[:], s, k * P, (A[0][:, k], A[1][:, k]), k == 0, k == KT - 1)
                            if n % 4 == 3:
                                mm.then_inc(to_act[4 + n // 4 % 2], 1)
                    pe.drain().then_inc(onehot.free, 1)
                    settle()
                def up():
                    for e in range(NB):
                        channel_tile(e, to_act)

                def down(b2):
                    slots = take(NB)
                    for half in range(2):
                        for part in (range(NB - 1), range(NB - 1, NB)) if half == 0 else (range(NB),):
                            for mi in range(4):
                                o = fill(4 + mi) if part[0] == 0 else bk[4 + mi]
                                for e in part:
                                    if half == 0 and mi == 0:
                                        pe.wait_ge(e_chan.ready, e_chan.to_read("pe"))
                                    mm = cols_of(o[:], slots[e], (4 * half + mi) * P,
                                                 (e_hi[:, b2, e], e_lo[:, b2, e]), e == 0, e == NB - 1)
                                if part[-1] == NB - 1:
                                    mm.then_inc(to_dve[4 + mi], 1)

                grow = [(e_chan._tally("pe"), 2 * NB)] + [(n_fill[b], 4) for b in range(4, 8)]
                up()
                settle()
                with repeat(pe, BLOCKS // 4, grow + [(units._tally("pe"), 2 * NB)]):
                    down(0)
                    down(1)
                    settle()
                down(0)
                up()
                down(1)
                settle()
                with repeat(pe, BLOCKS // 4 - 1, grow + [(units._tally("pe"), 4 * NB)] + [(n_fill[b], 2) for b in range(4)]):
                    for b2 in range(2):
                        up()
                        down(b2)
                    settle()
                pe.drain().then_inc(hid.free, 1)
                pe.wait_ge(p_split, L + 1)
                for u in range(2):
                    s = take()
                    for i in range(4):
                        b = ple_bank(4 * u + i)
                        o = fill(b)
                        for k in range(2):
                            mm = cols_of(o[:], s, (i * 2 + k) * P, (p_hi[:, k], p_lo[:, k]), k == 0, k == 1)
                        mm.then_inc(to_act[b], 1)
                    if u == 0:
                        norm()
                channel_tiles(KT, to_act)
                pe.drain().then_inc(hid.free, 1)
                if U_PAD:
                    take(U_PAD)
                settle()

        @block.scalar
        def _(act):
            def full(b):
                act.wait_ge(to_act[b], n_act[b].next())
                return bk[b]

            t = {n: Tally() for n in ("x", "hf", "ss", "taps", "dd", "ysq", "gate",
                                      "prod", "g_out0", "g_out1", "early0", "early1",
                                      "gate_out0", "gate_out1")}

            def norm(of_input=False):
                if of_input:
                    act.wait_ge(x_in, 16)
                for m in range(KT):
                    if not of_input:
                        act.wait_ge(x_new, t["x"].next())
                    act.wait_ge(squares.free, squares.to_write())
                    act.activation(sq[:, m % 2], x_res[:, m], ACT.Square).then_inc(squares.ready, 1)
                o = full(0)
                act.activation(rs[:], o[:], ACT.Sqrt, bias=EPS, scale=1.0 / D_MODEL).then_inc(rs_root, 1)
                act.drain().then_inc(bank_free[0], 1)
                act.wait_ge(hid.free, hid.to_write("act"))
                for m in range(KT):
                    act.wait_ge(hf_done, t["hf"].next())
                    act.activation(h_hi[:, m], hf[:, m % 2], ACT.Copy).then_inc(hh_done, 1)

            act.wait_ge(cst_in, 16)
            act.wait_ge(rope_arg, 1)
            act.activation(trig[:].rearrange("p a c r -> p (a c r)"), ang[:, 0:2].rearrange("p a n -> p (a n)"),
                           ACT.Sin).then_inc(trig_done, 1)
            for L in range(depth):
                def par(name, a=0, b=None, L=L):
                    lo, hi = PAR[name]
                    lo, hi = lo + a, hi if b is None else lo + b
                    return pn[:, L, lo:hi] if hi <= N_NORMS else pr[:, lo - N_NORMS:hi - N_NORMS]
                n_gate = [0]

                def put_gate(b, buf):
                    n, s = n_gate[0], n_gate[0] % 2
                    o = full(b)
                    act.wait_ge(gate_out[s], t[f"gate_out{s}"].next(16))
                    act.activation(buf[:, s], o[:], ACT.Sigmoid).then_inc(bank_free[b], 1)
                    act.drain()
                    act.dma_start(mix_dram[L, n], buf[:, s]).then_inc(gate_out[s], 16)
                    n_gate[0] += 1

                def gates_gone():
                    for s in range(2):
                        act.wait_ge(gate_out[s], t[f"gate_out{s}"].now() + 16)

                norm(of_input=L == 0)
                act.wait_ge(par_in, 16 * (L + 1))
                for n in range(GATE_AT[0] // 2):
                    put_gate(5 + n % 2, gate_i)
                act.wait_ge(dt_arg, L + 1)
                act.activation(dts[:, 1], dts[:, 0], ACT.Exp, scale=-1.0)
                act.activation(dts[:, 5, 0:SSM_HEADS], par("a_log"), ACT.Exp).then_inc(dt_exp, 1)
                for n in range(GATE_AT[0] // 2, GATE_AT[0]):
                    put_gate(5 + n % 2, gate_i)
                o = full(7)
                flat = {n: v[:].rearrange("p c h -> p (c h)") for n, v in dtb.items()}
                act.activation(flat["cs_tok"], o[:, 0:P], ACT.Copy)
                act.activation(flat["e_cs"], o[:, 0:P], ACT.Exp)
                act.activation(flat["c_dec"], o[:, P:2 * P], ACT.Exp).then_inc(cs_exp, 1)
                act.wait_ge(decay_arg, L + 1)
                act.activation(flat["decay"], dts[:, 0], ACT.Exp).then_inc(decay_done, 1)
                for n in range(5):
                    b = 5 + n % 2
                    o = full(b)
                    act.activation(qi_t[:, n] if n < 4 else ki_t[:], o[:], ACT.Copy).then_inc(qi_turned, 1)
                    act.drain().then_inc(bank_free[b], 1)
                for j in range(1, NT):
                    for h in range(IDX_HEADS):
                        o = full(h % 4)
                        act.wait_ge(relus.free, relus.to_write())
                        act.activation(relu[:, h % 2, 0:(j + 1) * P], o[:, 0:(j + 1) * P], ACT.Relu)\
                           .then_inc(relus.ready, 1)
                        act.drain().then_inc(bank_free[h % 4], 1)
                        if j > 1 and h == 1:
                            for n in range(GATE_AT[1] // 2):
                                put_gate(5 + n % 2, gate_i)
                act.wait_ge(relus.free, relus.all_read())
                gates_gone()
                for g in range(KV_HEADS):
                    for j in range(NT):
                        o = full(j)
                        act.wait_ge(qk_sq.free, qk_sq.to_write())
                        act.activation(sqq[:, 0:REP].rearrange("p h d -> p (h d)"), o[:], ACT.Square)\
                           .then_inc(qk_sq.ready, 1)
                    for j in range(NT):
                        o = full(4 + j)
                        act.activation(v_sb[:, j], o[:, P:2 * P], ACT.Copy)
                        act.wait_ge(qk_sq.free, qk_sq.to_write())
                        act.activation(sqq[:, REP], o[:, 0:P], ACT.Square).then_inc(qk_sq.ready, 1)
                    act.wait_ge(qk_ss, t["ss"].next())
                    act.activation(ssq[:].rearrange("p a b -> p (a b)"), ssq[:].rearrange("p a b -> p (a b)"), ACT.Sqrt,
                                   bias=EPS, scale=1.0 / ATT_D).then_inc(qk_root, 1)
                    for n in range(GATE_AT[2 + g]):
                        put_gate(GATE_BANKS[n], p_t)
                    for n in range(REP + 1):
                        o = full(n % 4)
                        act.activation(qk_t[:, n], o[:], ACT.Copy).then_inc(qk_turned, 1)
                        act.drain().then_inc(bank_free[n % 4], 1)
                    steps = [(h, j) for h in range(REP) for j in range(NT)]
                    for s in range(len(steps) + TO_VALUES):
                        if s < len(steps):
                            h, j = steps[s]
                            q, wd = s % 4, (j + 1) * P
                            act.wait_ge(scores.ready, scores.to_read("act"))
                            act.activation(sc[:, q, 0:wd], sc[:, q, 0:wd], ACT.Exp, bias=mx[:, q, 1:2],
                                           scale=ATT_D ** -0.5, accum_out=sm[:, q, 0:1]).then_inc(probs, 1)
                        if 0 <= s - TO_TURN < len(steps):
                            h, j = steps[s - TO_TURN]
                            b = 2 + s % 2
                            o = full(b)
                            if s == TO_TURN:
                                gates_gone()
                            act.wait_ge(p_turn.free, p_turn.to_write())
                            act.activation(p_t[:, (s - TO_TURN) % 2, 0:(j + 1) * P], o[:, 0:(j + 1) * P], ACT.Copy)\
                               .then_inc(p_turn.ready, 1)
                            act.drain().then_inc(bank_free[b], 1)
                            act.drain().then_inc(scores.free, 1)
                        if 0 <= s - TO_VALUES < len(steps) and steps[s - TO_VALUES][1] == NT - 1:
                            h = steps[s - TO_VALUES][0]
                            if h == 0:
                                act.wait_ge(a_chan.free, a_chan.to_write("act"))
                            o = full(4 + h % 2)
                            act.activation(a_hi[:, h], o[:], ACT.Copy).then_inc(a_high, 1)
                for g in range(GROUPS):
                    for n in range(CONV_TILES + 1):
                        if n < CONV_TILES:
                            i = g * CONV_TILES + n
                            o = full(n % 4)
                            if n == 0:
                                act.wait_ge(s_chan.free, s_chan.to_write("act"))
                            act.drain()
                            act.activation(acc[:, n % 2], o[:], ACT.Identity, bias=par("conv_b", i, i + 1),
                                           scale=par("conv_w", i * CONV_W + 3, i * CONV_W + 4)).then_inc(tap0, 1)
                        if n >= 1:
                            m = n - 1
                            act.wait_ge(taps, t["taps"].next())
                            act.wait_ge(conv_out.free, conv_out.to_write())
                            dst = b_t[:] if m == 0 else c_t[:] if m == 1 else xs_t[:, m % 2]
                            act.activation(dst, acc[:, m % 2], ACT.Silu).then_inc(conv_out.ready, 1)
                            if m == 2:
                                o = full(4)
                                act.activation(b_tok[:].rearrange("p c n -> p (c n)"), o[:], ACT.Copy)\
                                   .then_inc(btok_done, 1)
                                act.drain().then_inc(bank_free[4], 1)

                    def silu_z(j):
                        o = full(Z_BANKS[j])
                        act.activation(sz[:, j], o[:], ACT.Silu).then_inc(sz_done, 1)
                        act.drain().then_inc(bank_free[Z_BANKS[j]], 1)

                    silu_z(0)
                    for r in range(R_HEADS):
                        act.wait_ge(diff, t["dd"].next())
                        act.activation(dd[:, r % 2], dd[:, r % 2], ACT.Exp).then_inc(expd, 1)
                        if r == 4:
                            silu_z(1)
                    silu_z(2)
                    for c in range(NT):
                        if c == 2:
                            silu_z(3)
                        act.wait_ge(y_sq, t["ysq"].next())
                        act.activation(acc[:, 1], yy[:, c], ACT.Square, accum_out=sss[:, c:c + 1])
                        act.drain()
                    act.activation(sss[:], sss[:], ACT.Sqrt, bias=EPS, scale=1.0 / GW).then_inc(y_root, 1)
                    for i in range(4):
                        o = full(4 + i % 2)
                        k = g * 4 + i
                        act.activation(s_hi[:, i], o[:], ACT.Copy, scale=par("ssm_norm", k, k + 1)).then_inc(s_high, 1)
                md = mix_dram[L].rearrange("(m two) p t -> m p two t", two=2)
                act.wait_ge(hid.free, hid.to_write("act"))
                for m in range(-GATE_BUFS, KT):
                    if m >= 0:
                        act.wait_ge(hf_done, t["hf"].next())
                        act.activation(h_hi[:, m], y_att[:, m], ACT.Copy).then_inc(hh_done, 1)
                    if m + GATE_BUFS < KT:
                        q = m + GATE_BUFS
                        act.wait_ge(gate_s.free, gate_s.to_write())
                        act.dma_start(gate_t[:, q % GATE_BUFS], md[q]).then_inc(gate_landed[q % GATE_BUFS], 16)
                act.wait_ge(x_new, t["x"].now() + 1)
                act.dma_start(key_sb[:], keys[L]).then_inc(key_in, 16)
                if L + 1 < depth:
                    act.dma_start(pr[:], params[:, L + 1, N_NORMS:]).then_inc(par_in, 16)
                norm()
                for n in range(2 * PEER_HEADS):
                    o = full(n % 4)
                    act.activation(pq_t[:, n], o[:], ACT.Copy).then_inc(pq_done, 1)
                    act.drain().then_inc(bank_free[n % 4], 1)

                def put_early(tile, n):
                    o = full(4 + n % 2)
                    act.wait_ge(early_out[n % 2], t[f"early{n % 2}"].next(16))
                    act.activation(early[:, n % 2], o[:], ACT.Gelu).then_inc(bank_free[4 + n % 2], 1)
                    act.drain()
                    act.dma_start(early_dram[L, tile], early[:, n % 2]).then_inc(early_out[n % 2], 16)

                def key_scores():
                    act.wait_ge(ps_done.free, ps_done.to_write())
                    for q in range(4):
                        o = full(q)
                        mm = act.activation(ps[:, 4 * q:4 * q + 4].rearrange("p a b -> p (a b)"), o[:], ACT.Copy)
                        if q == 3:
                            mm.then_inc(ps_done.ready, 1)
                        act.drain().then_inc(bank_free[q], 1)

                key_scores()
                per_j = EARLY // 2 // NT
                for j in range(NT):
                    for u in range(per_j):
                        if u == 4 and j + 1 < NT:
                            key_scores()
                        if u == per_j - 1:
                            act.wait_ge(gate_arg, t["gate"].next())
                            act.activation(cv[:].rearrange("p h k -> p (h k)"), sel[:, 2].rearrange("p h k -> p (h k)"),
                                           ACT.Exp).then_inc(gate_exp, 1)
                        put_early(j * per_j + u, u)
                    o = full(6)
                    act.activation(sel_t[:, :, j * P:(j + 1) * P], o[:, 0:3 * P].rearrange("p (i t) -> p i t", i=3),
                                   ACT.Copy).then_inc(sel_turned, 1)
                    act.drain().then_inc(bank_free[6], 1)
                with repeat(act, SEQ // TB // STEPS, [(n_act[b], STEPS // 4) for b in range(4)]
                            + [(n_act[b], U_LOOP // 2) for b in (4, 5)] + [(t[f"g_out{s}"], 16 * FILLS // 2) for s in range(2)]
                            + [(t["early0"], 16 * U_LOOP // 2), (t["early1"], 16 * U_LOOP // 2)]) as i:
                    for n in range(STEPS):
                        b, f, at = n % 4, n * TB // GRP, n * TB % GRP
                        s = f % 2
                        if at == 0:
                            act.wait_ge(g_out[s], t[f"g_out{s}"].next(16))
                        o = full(b)
                        act.activation(gbuf[:, s, :, at:at + TB].rearrange("p k t -> p t k"),
                                       o[:].rearrange("p (t k) -> p t k", t=TB), ACT.Copy).then_inc(bank_free[b], 1)
                        if at == GRP - TB:
                            act.drain()
                            act.dma_start(gates_dram[L, i * FILLS + f], gbuf[:, s]).then_inc(g_out[s], 16)
                        if n % 4 == 3:
                            put_early(i * U_LOOP + (EARLY // 2 + n // 4), n // 4)
                for s in range(2):
                    act.wait_ge(g_out[s], t[f"g_out{s}"].now() + 16)
                    act.wait_ge(early_out[s], t[f"early{s}"].now() + 16)
                gd = gates_dram[L].rearrange("g p (b e) t -> b p g e t", e=NB)
                ed = early_dram[L].rearrange("(b e) p t -> b p e t", e=NB)

                def load(b2, block, with_early):
                    act.wait_ge(g_load.free, g_load.to_write())
                    act.dma_start(g_in[:, b2], gd[block]).then_inc(g_landed[b2], 16)
                    if with_early:
                        act.dma_start(back[:, b2], ed[block]).then_inc(back_landed[b2], 16)

                def high(b2, e, value):
                    act.wait_ge(e_prod, t["prod"].next())
                    act.wait_ge(e_chan.free, e_chan.to_write("act"))
                    act.activation(e_hi[:, b2, e], value, ACT.Copy).then_inc(e_high, 1)

                def pair(i, first, was_early, ahead, early_ahead):
                    for b2 in range(2):
                        for e in range(NB):
                            if was_early:
                                high(b2, e, back[:, b2, e])
                                continue
                            o = full(e)
                            act.wait_ge(gelus.free, gelus.to_write())
                            act.activation(gel[:, e % 2], o[:], ACT.Gelu).then_inc(gelus.ready, 1)
                            act.drain().then_inc(bank_free[e], 1)
                            high(b2, e, gel[:, e % 2])
                        if ahead:
                            load(b2, i * 2 + (first + b2 + 2), early_ahead)

                for b2 in range(2):
                    load(b2, b2, True)
                half = BLOCKS // 4
                grow = [(g_load._tally("writer"), 2), (e_chan._tally("act"), 2 * NB), (t["prod"], 2 * NB)]
                more = [(n_act[b], 2) for b in range(NB)] + [(gelus._tally("writer"), 2 * NB)]
                with repeat(act, half - 1, grow) as i:
                    pair(i, 0, True, True, True)
                pair(half - 1, 0, True, True, False)
                act.dma_start(pf[:], p_emb[L]).then_inc(p_in, 16)
                with repeat(act, half - 1, grow + more) as i:
                    pair(i, BLOCKS // 2, False, True, False)
                act.wait_ge(p_in, 16 * (L + 1))
                act.activation(p_hi[:].rearrange("p a n -> p (a n)"), pf[:].rearrange("p a n -> p (a n)"), ACT.Copy)\
                   .then_inc(p_high, 1)
                pair(half - 1, BLOCKS // 2, False, False, False)
                for m in range(KT):
                    if m == 4:
                        norm()
                    o = full(ple_bank(m))
                    act.activation(pp[:, m], o[:], ACT.Copy).then_inc(pp_done, 1)
                    act.drain().then_inc(bank_free[ple_bank(m)], 1)
                for m in range(KT):
                    o = full(m % 4)
                    act.wait_ge(pg_chan.free, pg_chan.to_write())
                    act.activation(pg[:, m % 2], o[:], ACT.Sigmoid).then_inc(pg_chan.ready, 1)
                    act.drain().then_inc(bank_free[m % 4], 1)

        @block.vector
        def _(dve):
            def full(b):
                dve.wait_ge(to_dve[b], n_dve[b].next())
                return bk[b]

            def bc(ap, axis, shape):
                return ap.unsqueeze(axis).broadcast_to(shape)

            t = {n: Tally() for n in ("rs", "hh", "dtexp", "cs", "qroot", "probs", "ahigh", "tap0", "exp", "yroot",
                                      "shigh", "gexp", "ehigh", "sz", "land0", "land1", "back0", "back1")}
            t_landed = [Tally() for _ in range(GATE_BUFS)]

            def low(hi_sem, key, hi, lo, full_value):
                dve.wait_ge(hi_sem, t[key].next())
                return dve.tensor_tensor(lo, full_value, hi.bitcast(F32), ALU.subtract)

            def norm(g):
                dve.wait_ge(rs_root, t["rs"].next())
                dve.reciprocal(rs[:], rs[:])
                dve.drain()
                for m in range(KT + 1):
                    if m < KT:
                        dve.scalar_tensor_tensor(hf[:, m % 2], x_res[:, m], g[:, m:m + 1], rs[:], ALU.mult, ALU.mult)\
                           .then_inc(hf_done, 1)
                        dve.drain()
                    if m >= 1:
                        q = m - 1
                        low(hh_done, "hh", h_hi[:, q], h_lo[:, q], hf[:, q % 2]).then_inc(hid.ready, 1)
                        dve.drain()

            def rope(x1, x2, c, s, tm, o1, o2):
                dve.drain()
                dve.tensor_tensor(tm[0], x1, c, ALU.mult)
                dve.tensor_tensor(tm[1], x2, s, ALU.mult)
                dve.tensor_tensor(tm[2], x1, s, ALU.mult)
                dve.tensor_tensor(tm[3], x2, c, ALU.mult)
                dve.drain()
                dve.tensor_tensor(o1, tm[0], tm[1], ALU.subtract)
                return dve.tensor_tensor(o2, tm[2], tm[3], ALU.add)

            dve.wait_ge(pos_in, 16)
            dve.wait_ge(cst_in, 16)
            dve.tensor_copy(pos_f[:], pos_i[:])
            dve.drain()
            a3 = [ang[:, i].rearrange("p (c r) -> p c r", c=NT) for i in range(3)]
            dve.tensor_tensor(a3[0], bc(pos_f[:], 2, [P, NT, ROPE]), bc(inv, 1, [P, NT, ROPE]), ALU.mult)
            dve.drain()
            dve.tensor_scalar(ang[:, 1], ang[:, 0], 1.0 / (2 * np.pi), MAGIC, ALU.mult, ALU.add)
            dve.drain()
            dve.tensor_scalar(ang[:, 1], ang[:, 1], -MAGIC, None, ALU.add)
            dve.drain()
            for c in TWO_PI:
                dve.scalar_tensor_tensor(ang[:, 0], ang[:, 1], -c, ang[:, 0], ALU.mult, ALU.add)
                dve.drain()
            EDGE = 3.1415925
            dve.tensor_scalar(ang[:, 1], ang[:, 0], np.pi / 2, None, ALU.add)
            dve.drain()
            dve.tensor_scalar(ang[:, 2], ang[:, 1], np.pi, -2 * np.pi, ALU.is_gt, ALU.mult)
            dve.drain()
            dve.tensor_tensor(ang[:, 1], ang[:, 1], ang[:, 2], ALU.add)
            dve.drain()
            dve.tensor_scalar(ang[:, 0], ang[:, 0], EDGE, -EDGE, ALU.min, ALU.max)
            dve.tensor_scalar(ang[:, 1], ang[:, 1], EDGE, -EDGE, ALU.min, ALU.max).then_inc(rope_arg, 1)
            dve.wait_ge(trig_done, 1)
            dve.wait_ge(norms_in, 16)
            dve.wait_ge(x_in, 16)
            dve.wait_ge(zero_set, 1)
            for L in range(depth):
                def par(name, a=0, b=None, L=L):
                    lo, hi = PAR[name]
                    lo, hi = lo + a, hi if b is None else lo + b
                    return pn[:, L, lo:hi] if hi <= N_NORMS else pr[:, lo - N_NORMS:hi - N_NORMS]
                norm(par("norm_mix"))
                dve.wait_ge(par_in, 16 * (L + 1))
                half = IDX_D // 2
                for j in range(NT):
                    v = full(j)[:].rearrange("p (h two d) -> p h two d", h=IDX_HEADS, two=2)
                    q = qi[:, j].rearrange("p (h two d) -> p h two d", h=IDX_HEADS, two=2)
                    sh = [P, IDX_HEADS, half]
                    tm = [rt[:, i].rearrange("p (h d) -> p h d", h=IDX_HEADS) for i in range(4)]
                    rope(v[:, :, 0], v[:, :, 1], bc(cos_i[:, j], 1, sh), bc(sin_i[:, j], 1, sh), tm,
                         q[:, :, 0], q[:, :, 1]).then_inc(qi_rope, 1)
                    dve.drain().then_inc(bank_free[j], 1)
                dve.tensor_copy(small[:].rearrange("p c n -> p (c n)"), full(4)[:])
                dve.drain().then_inc(bank_free[4], 1)
                tm = [rt[:, i, 0:NT * half].rearrange("p (c d) -> p c d", c=NT) for i in range(4)]
                rope(small[:, :, 0:half], small[:, :, half:2 * half], cos_i, sin_i, tm, kid[:, :, 0:half],
                     kid[:, :, half:IDX_D])
                dve.drain()
                dve.tensor_copy(kid[:, :, IDX_D:], kid[:, :, 0:IDX_D]).then_inc(qi_rope, 1)
                dve.tensor_scalar(wi[:], small[:, :, IDX_D:IDX_D + IDX_HEADS], IDX_D ** -0.5, IDX_HEADS ** -0.5,
                                  ALU.mult, ALU.mult)
                H0 = IDX_D + IDX_HEADS
                f = [dts[:, i] for i in range(6)]
                g3 = [v.rearrange("p (c h) -> p c h", c=NT) for v in f]
                sh = [P, NT, SSM_HEADS]
                dve.tensor_tensor(g3[2], small[:, :, H0:H0 + SSM_HEADS], bc(par("dt_bias"), 1, sh), ALU.add)
                dve.drain()
                dve.scalar_tensor_tensor(f[0], f[2], -1.0, f[2], ALU.mult, ALU.max).then_inc(dt_arg, 1)
                dve.drain()
                dve.tensor_scalar(f[2], f[2], 0.0, None, ALU.max)
                dve.wait_ge(dt_exp, t["dtexp"].next())
                dve.tensor_scalar(f[3], f[1], 2.0, None, ALU.add)
                dve.drain()
                dve.reciprocal(f[3], f[3])
                dve.drain()
                dve.tensor_tensor(f[3], f[1], f[3], ALU.mult)
                dve.drain()
                dve.tensor_tensor(f[1], f[3], f[3], ALU.mult)
                dve.drain()
                dve.tensor_scalar(f[4], f[1], 1.0 / 17, None, ALU.mult)
                dve.drain()
                for d in (15, 13, 11, 9, 7, 5, 3):
                    dve.scalar_tensor_tensor(f[4], f[4], 1.0 / d, f[1], ALU.add, ALU.mult)
                    dve.drain()
                dve.scalar_tensor_tensor(f[4], f[4], 1.0, f[3], ALU.add, ALU.mult)
                dve.drain()
                dtf = dtb["dt"][:].rearrange("p c h -> p (c h)")
                dve.scalar_tensor_tensor(dtf, f[4], 2.0, f[2], ALU.mult, ALU.add)
                dve.drain()
                dve.scalar_tensor_tensor(dtb["adt"][:], dtb["dt"][:], -1.0, bc(f[5][:, 0:SSM_HEADS], 1, sh), ALU.mult,
                                         ALU.mult).then_inc(adt_done, 1)
                dve.wait_ge(cs_exp, t["cs"].next())
                dve.tensor_tensor(f[0], bk[7][:, P:2 * P], dtb["cs_tok"][:].rearrange("p c h -> p (c h)"), ALU.subtract)
                dve.drain().then_inc(bank_free[7], 1)
                dve.drain().then_inc(decay_arg, 1)
                for j in range(1, NT):
                    wd = (j + 1) * P
                    I = score[:, 0:wd]
                    for h in range(IDX_HEADS):
                        dve.wait_ge(relus.ready, relus.to_read("dve"))
                        r = relu[:, h % 2, 0:wd]
                        if h == 0:
                            mm = dve.tensor_scalar(I, r, wi[:, j, 0:1], None, ALU.mult)
                        else:
                            mm = dve.scalar_tensor_tensor(I, r, wi[:, j, h:h + 1], I, ALU.mult, ALU.add)
                        mm.then_inc(relus.free, 1)
                        dve.drain()
                    dve.tensor_tensor(score[:, j * P:wd], score[:, j * P:wd], causal, ALU.add)
                    dve.drain()
                    for _ in range(TOPK // 8):
                        dve.max(top8[:], I)
                        dve.drain()
                        dve.match_replace(I, top8[:], I, GONE)
                        dve.drain()
                    dve.tensor_scalar(bias[:, OFF[j]:OFF[j] + wd], I, -2e38, BIG, ALU.is_gt, ALU.mult)
                    dve.drain()
                dve.tensor_copy(bias[:, 0:P], causal)
                for g in range(KV_HEADS):
                    for heads in (slice(0, REP), slice(REP, REP + 1)):
                        for j in range(NT):
                            dve.wait_ge(qk_sq.ready, qk_sq.to_read("dve"))
                            dve.tensor_reduce(ssq[:, j, heads], sqq[:, heads], AX.X, ALU.add).then_inc(qk_sq.free, 1)
                    dve.drain().then_inc(qk_ss, 1)
                    dve.wait_ge(qk_root, t["qroot"].next())
                    ss2 = ssq[:].rearrange("p a b -> p (a b)")
                    dve.reciprocal(ss2, ss2)
                    dve.drain()
                    for j in range(NT):
                        o, o2 = bk[j], bk[4 + j]
                        if j == 0:
                            dve.wait_ge(a_chan.free, g + 1 + L * KV_HEADS)
                        for h in range(REP):
                            mm = dve.scalar_tensor_tensor(qk[:, j, h], o[:, h * ATT_D:(h + 1) * ATT_D], ssq[:, j, h:h + 1],
                                                          par("q_norm"), ALU.mult, ALU.mult)
                        mm.then_inc(bank_free[j], 1)
                        dve.scalar_tensor_tensor(qk[:, j, REP], o2[:, 0:P], ssq[:, j, REP:REP + 1], par("k_norm"),
                                                 ALU.mult, ALU.mult).then_inc(bank_free[4 + j], 1)
                        v = qk[:, j].rearrange("p h (two d) -> p h two d", two=2)
                        sh = [P, REP + 1, ATT_D // 2]
                        tm = [rt2[:, i].rearrange("p (h d) -> p h d", h=REP + 1) for i in range(4)]
                        mm = rope(v[:, :, 0], v[:, :, 1], bc(cos_a[:, j], 1, sh), bc(sin_a[:, j], 1, sh), tm,
                                  v[:, :, 0], v[:, :, 1])
                        if j == NT - 1:
                            mm.then_inc(qk_rope, 1)
                        dve.drain()
                    steps = [(h, j) for h in range(REP) for j in range(NT)]
                    for s in range(len(steps) + TO_VALUES):
                        if s < len(steps):
                            h, j = steps[s]
                            q, wd = s % 4, (j + 1) * P
                            o = full(s % 2)
                            dve.wait_ge(scores.free, scores.to_write())
                            dve.tensor_tensor_reduce(out=sc[:, q, 0:wd], in0=o[:, 0:wd], in1=bias[:, OFF[j]:OFF[j] + wd],
                                                     scale=1.0, scalar=GONE, op0=ALU.add, op1=ALU.max,
                                                     accum_out=mx[:, q, 0:1])
                            dve.drain().then_inc(bank_free[s % 2], 1)
                            dve.tensor_scalar(mx[:, q, 1:2], mx[:, q, 0:1], -(ATT_D ** -0.5), None, ALU.mult)\
                               .then_inc(scores.ready, 1)
                        if 0 <= s - 1 < len(steps):
                            h, j = steps[s - 1]
                            q, wd = (s - 1) % 4, (j + 1) * P
                            dve.wait_ge(probs, t["probs"].next())
                            dve.reciprocal(sm[:, q, 1:2], sm[:, q, 0:1])
                            dve.drain()
                            dve.tensor_scalar(sc[:, q, 0:wd], sc[:, q, 0:wd], sm[:, q, 1:2], None, ALU.mult)\
                               .then_inc(probs_n, 1)
                        if 0 <= s - TO_VALUES < len(steps) and steps[s - TO_VALUES][1] == NT - 1:
                            h = steps[s - TO_VALUES][0]
                            o = bk[4 + h % 2]
                            low(a_high, "ahigh", a_hi[:, h], a_lo[:, h], o[:]).then_inc(bank_free[4 + h % 2], 1)
                            if h == REP - 1:
                                dve.drain().then_inc(a_chan.ready, 1)
                    for m in range(KT):
                        o = full(6 + m % 2)
                        if g == 0:
                            mm = dve.tensor_copy(y_att[:, m], o[:])
                        else:
                            mm = dve.tensor_tensor(y_att[:, m], y_att[:, m], o[:], ALU.add)
                        mm.then_inc(bank_free[6 + m % 2], 1)
                    dve.drain().then_inc(a_chan.free, 1)
                dve.wait_ge(decay_done, L + 1)
                for g in range(GROUPS):
                    for n in range(CONV_TILES + 3):
                        if n < CONV_TILES:
                            i = (g * CONV_TILES + n) * CONV_W
                            o = bk[n % 4]
                            dve.wait_ge(tap0, t["tap0"].next())
                            a = acc[:, n % 2]
                            for d in range(1, CONV_W):
                                mm = dve.scalar_tensor_tensor(a[:, d:], o[:, 0:SEQ - d],
                                                              par("conv_w", i + CONV_W - 1 - d, i + CONV_W - d), a[:, d:],
                                                              ALU.mult, ALU.add)
                                dve.drain()
                            dve.drain().then_inc(taps, 1)
                            dve.drain().then_inc(bank_free[n % 4], 1)
                        m = n - 3
                        if m == 1:
                            o = full(6)
                            dve.tensor_tensor(cb[:], o[:].rearrange("p (c l) -> p c l", c=NT),
                                              bc(tri, 1, [P, NT, P]), ALU.mult).then_inc(bank_free[6], 1)
                        if m >= 2:
                            q = m - 2
                            o = full(4 + m % 2)[:].rearrange("p (c h d) -> p c h d", c=NT, h=2)
                            hs = slice(g * R_HEADS + 2 * q, g * R_HEADS + 2 * q + 2)
                            sh = [P, NT, 2, HEAD_P]
                            dst = xdt[:, :, q * P:(q + 1) * P].rearrange("p c (h d) -> p c h d", h=2)
                            dst2 = yy[:, :, q * P:(q + 1) * P].rearrange("p c (h d) -> p c h d", h=2)
                            dve.tensor_tensor(dst, o, bc(dtb["dt"][:, :, hs], 3, sh), ALU.mult).then_inc(xdt_done, 1)
                            dve.tensor_tensor(dst2, o, bc(par("d_skip", hs.start, hs.stop), 1, [P, NT, 2])
                                              .unsqueeze(3).broadcast_to(sh), ALU.mult)\
                               .then_inc(bank_free[4 + m % 2], 1)
                    for r in range(R_HEADS + 1):
                        if r < R_HEADS:
                            hh = g * R_HEADS + r
                            o = full(4 + r % 2)
                            dve.wait_ge(mt.free, mt.to_write())
                            d3 = dd[:, r % 2].rearrange("p (c l) -> p c l", c=NT)
                            dve.tensor_tensor(d3, o[:].rearrange("p (c l) -> p c l", c=NT),
                                              dtb["cs_tok"][:, :, hh:hh + 1].broadcast_to([P, NT, P]), ALU.subtract)\
                               .then_inc(bank_free[4 + r % 2], 1)
                            dve.drain()
                            dve.tensor_scalar(dd[:, r % 2], dd[:, r % 2], 0.0, None, ALU.min).then_inc(diff, 1)
                        if r >= 1:
                            q = (r - 1) % 2
                            dve.wait_ge(expd, t["exp"].next())
                            dve.tensor_tensor(dd[:, q], dd[:, q], cb[:].rearrange("p c l -> p (c l)"), ALU.mult)\
                               .then_inc(mt.ready, 1)
                    hs = slice(g * R_HEADS, (g + 1) * R_HEADS)
                    sh = [P, R_HEADS, HEAD_P]
                    for c in range(NT):
                        if c < NT - 1:
                            dve.tensor_tensor(acc[:, 0].rearrange("p (h d) -> p h d", h=R_HEADS),
                                              xdt[:, c].rearrange("p (h d) -> p h d", h=R_HEADS),
                                              bc(dtb["decay"][:, c, hs], 2, sh), ALU.mult).then_inc(xdec_done, 1)
                        o = full(c)
                        dve.tensor_tensor(yy[:, c], yy[:, c], o[:], ALU.add).then_inc(bank_free[c], 1)
                        if c > 0:
                            o = full(7)
                            dve.tensor_tensor(dd[:, 0].rearrange("p (h d) -> p h d", h=R_HEADS),
                                              o[:].rearrange("p (h d) -> p h d", h=R_HEADS),
                                              bc(dtb["e_cs"][:, c, hs], 2, sh), ALU.mult).then_inc(bank_free[7], 1)
                            dve.drain()
                            dve.tensor_tensor(yy[:, c], yy[:, c], dd[:, 0], ALU.add)
                        dve.drain()
                        dve.wait_ge(sz_done, t["sz"].next())
                        dve.tensor_tensor(yy[:, c], yy[:, c], sz[:, c], ALU.mult).then_inc(y_sq, 1)
                        if c < NT - 1:
                            o = full(6)
                            if c == 0:
                                mm = dve.tensor_copy(prev[:], o[:])
                            else:
                                pv3 = prev[:].rearrange("p (h d) -> p h d", h=R_HEADS)
                                dve.tensor_tensor(pv3, pv3, bc(dtb["c_dec"][:, c, hs], 2, sh), ALU.mult)
                                dve.drain()
                                mm = dve.tensor_tensor(prev[:], prev[:], o[:], ALU.add)
                            mm.then_inc(state_done, 1)
                            dve.drain().then_inc(bank_free[6], 1)
                    dve.wait_ge(y_root, t["yroot"].next())
                    dve.reciprocal(sss[:], sss[:])
                    dve.drain()
                    for c in range(NT):
                        mm = dve.tensor_scalar(yy[:, c], yy[:, c], sss[:, c:c + 1], None, ALU.mult)
                    dve.drain().then_inc(y_norm, 1)
                    for i in range(4):
                        o = bk[4 + i % 2]
                        k = g * 4 + i
                        dve.wait_ge(s_high, t["shigh"].next())
                        dve.scalar_tensor_tensor(s_lo[:, i], o[:], par("ssm_norm", k, k + 1), s_hi[:, i].bitcast(F32),
                                                 ALU.mult, ALU.subtract).then_inc(bank_free[4 + i % 2], 1)
                    dve.drain().then_inc(s_chan.ready, 1)
                    for m in range(KT + 1):
                        if m < KT:
                            o = full(6 + m % 2)
                            if g == 0:
                                mm = dve.tensor_copy(y_ssm[:, m], o[:])
                            else:
                                mm = dve.tensor_tensor(y_ssm[:, m], y_ssm[:, m], o[:], ALU.add)
                            mm.then_inc(bank_free[6 + m % 2], 1)
                            if m == KT - 1:
                                dve.drain().then_inc(s_chan.free, 1)
                        if g < GROUPS - 1:
                            continue
                        if m < KT:
                            b = m % GATE_BUFS
                            dve.wait_ge(gate_landed[b], t_landed[b].next(16))
                            dve.tensor_tensor(y_att[:, m], y_att[:, m], gate_t[:, b, 0], ALU.mult)
                            dve.drain()
                            dve.tensor_tensor(y_ssm[:, m], y_ssm[:, m], gate_t[:, b, 1], ALU.mult).then_inc(gate_s.free, 1)
                            dve.drain()
                            dve.tensor_tensor(y_att[:, m], y_att[:, m], y_ssm[:, m], ALU.add).then_inc(hf_done, 1)
                        if m >= 1:
                            dve.drain()
                            low(hh_done, "hh", h_hi[:, m - 1], h_lo[:, m - 1], y_att[:, m - 1]).then_inc(hid.ready, 1)
                for m in range(KT):
                    o = full(m % 4)
                    dve.tensor_tensor(x_res[:, m], x_res[:, m], o[:], ALU.add).then_inc(bank_free[m % 4], 1)
                    dve.drain().then_inc(x_new, 1)
                norm(par("norm_ffn"))
                for j in range(NT):
                    dve.wait_ge(ps_done.ready, ps_done.to_read("dve"))
                    for n in range(2 * PEER_HEADS):
                        dve.max(pv[:, n, 0:8], ps[:, n])
                    dve.drain()
                    for n in range(2 * PEER_HEADS):
                        dve.max_index(pi[:, n, 0:8], pv[:, n, 0:8], ps[:, n])
                        dve.match_replace(ps[:, n], pv[:, n, 0:8], ps[:, n], GONE)
                    dve.drain()
                    for n in range(2 * PEER_HEADS):
                        dve.max(pv[:, n, 8:16], ps[:, n])
                    dve.drain()
                    for n in range(2 * PEER_HEADS):
                        mm = dve.max_index(pi[:, n, 8:16], pv[:, n, 8:16], ps[:, n])
                    mm.then_inc(ps_done.free, 1)
                    dve.drain()
                    dve.tensor_copy(pif[:], pi[:])
                    pv4 = pv[:].rearrange("p (h two) k -> p h two k", two=2)
                    pi4 = pif[:].rearrange("p (h two) k -> p h two k", two=2)
                    sh = [P, PEER_HEADS, PEER_K, PEER_K]
                    dve.tensor_tensor(cand[:].rearrange("p h (i j) -> p h i j", i=PEER_K), bc(pv4[:, :, 0], 3, sh),
                                      bc(pv4[:, :, 1], 2, sh), ALU.add)
                    dve.drain()
                    for h in range(PEER_HEADS):
                        dve.max(cv[:, h, 0:8], cand[:, h])
                    dve.drain()
                    for h in range(PEER_HEADS):
                        dve.max_index(ci[:, 0, h, 0:8], cv[:, h, 0:8], cand[:, h])
                        dve.match_replace(cand[:, h], cv[:, h, 0:8], cand[:, h], GONE)
                    dve.drain()
                    for h in range(PEER_HEADS):
                        dve.max(cv[:, h, 8:16], cand[:, h])
                    dve.drain()
                    for h in range(PEER_HEADS):
                        dve.max_index(ci[:, 0, h, 8:16], cv[:, h, 8:16], cand[:, h])
                    dve.drain()
                    shk = [P, PEER_HEADS, PEER_K]
                    dve.wait_ge(sel_done.free, sel_done.to_write())
                    dve.tensor_tensor(sel[:, 2], cv[:], cv[:, :, 0:1].broadcast_to(shk), ALU.subtract)\
                       .then_inc(gate_arg, 1)
                    dve.tensor_scalar(ci[:, 1], ci[:, 0], 4, None, ALU.logical_shift_right)
                    dve.tensor_scalar(ci[:, 2], ci[:, 0], PEER_K - 1, None, ALU.bitwise_and)
                    dve.drain()
                    dve.tensor_copy(cif[:], ci[:, 1:3])
                    dve.drain()
                    for q in range(2):
                        it = iota[:, 0:PEER_K].unsqueeze(1).broadcast_to([P, PEER_K, PEER_K]).unsqueeze(1).broadcast_to(sh)
                        dve.tensor_tensor(hot, bc(cif[:, q], 3, sh), it, ALU.is_equal)
                        dve.drain()
                        dve.tensor_tensor(hot, hot, bc(pi4[:, :, q], 2, sh), ALU.mult)
                        dve.drain()
                        dve.tensor_reduce(sel[:, q], hot, AX.X, ALU.add)
                        dve.drain()
                    dve.wait_ge(gate_exp, t["gexp"].next())
                    dve.tensor_reduce(psum8[:], cv[:], AX.X, ALU.add)
                    dve.drain()
                    dve.reciprocal(psum8[:], psum8[:])
                    dve.drain()
                    dve.tensor_tensor(sel[:, 2], cv[:], bc(psum8[:], 2, shk), ALU.mult)
                    dve.drain().then_inc(sel_done.ready, 1)
                dve.wait_ge(sel_turned, NT * (L + 1))
                with repeat(dve, SEQ // (ROWS * TB), [(onehot._tally("writer"), ROWS)]) as i:
                    for b in range(ROWS):
                        dve.wait_ge(onehot.free, onehot.to_write())
                        at = i * (ROWS * TB) + b * TB
                        sh = [P, TB, N_KEYS]
                        dve.tensor_tensor(rows[:, b, 1], bc(iota, 1, sh), bc(sel_t[:, 1, bass.ds(at, TB)], 2, sh),
                                          ALU.is_equal)
                        for k in range(TB):
                            one = bass.ds(at + k, 1)
                            mm = dve.tensor_scalar(rows[:, b, 0, k], iota, sel_t[:, 0, one], sel_t[:, 2, one],
                                                   ALU.is_equal, ALU.mult)
                        dve.drain().then_inc(onehot.ready, 1)
                def gated(b2, was_early):
                    dve.wait_ge(g_landed[b2], t[f"land{b2}"].next(16))
                    if was_early:
                        dve.wait_ge(back_landed[b2], t[f"back{b2}"].next(16))
                    lag = 1 if was_early else 0
                    for e in range(NB + lag):
                        if e < NB:
                            v = back[:, b2, e] if was_early else gel[:, e % 2]
                            if not was_early:
                                dve.wait_ge(gelus.ready, gelus.to_read("dve"))
                            v3 = v.rearrange("p (g t) -> p g t", g=N_GRP)
                            dve.tensor_tensor(v3, v3, g_in[:, b2, :, e], ALU.mult).then_inc(e_prod, 1)
                            dve.drain()
                        if e >= lag:
                            q = e - lag
                            v = back[:, b2, q] if was_early else gel[:, q % 2]
                            low(e_high, "ehigh", e_hi[:, b2, q], e_lo[:, b2, q], v).then_inc(e_chan.ready, 1)
                            if not was_early:
                                dve.drain().then_inc(gelus.free, 1)
                    dve.drain().then_inc(g_load.free, 1)

                def add_down(last=False):
                    for m in range(KT):
                        o = full(4 + m % 4)
                        dve.tensor_tensor(x_res[:, m], x_res[:, m], o[:], ALU.add).then_inc(bank_free[4 + m % 4], 1)
                        if last:
                            dve.drain().then_inc(x_new, 1)
                    dve.drain().then_inc(e_chan.free, NB)

                half = BLOCKS // 4
                grow = [(n_dve[b], 4) for b in range(4, 8)] + [(t["ehigh"], 2 * NB), (t["land0"], 16), (t["land1"], 16)]
                gated(0, True)
                with repeat(dve, half - 1, grow + [(t["back0"], 16), (t["back1"], 16)]):
                    for b2 in range(2):
                        gated(1 - b2, True)
                        add_down()
                gated(1, True)
                add_down()
                add_down()
                with repeat(dve, half - 1, grow + [(gelus._tally("dve"), 2 * NB)]):
                    for b2 in range(2):
                        gated(b2, False)
                        add_down()
                dve.wait_ge(p_high, L + 1)
                dve.tensor_tensor(p_lo[:].rearrange("p a n -> p (a n)"), pf[:].rearrange("p a n -> p (a n)"),
                                  p_hi[:].rearrange("p a n -> p (a n)").bitcast(F32), ALU.subtract).then_inc(p_split, 1)
                for b2 in range(2):
                    gated(b2, False)
                    add_down(last=b2 == 1)
                norm(par("norm_ple"))
                dve.wait_ge(pp_done, KT * (L + 1))
                for m in range(KT):
                    dve.wait_ge(pg_chan.ready, pg_chan.to_read("dve"))
                    dve.tensor_tensor(pg[:, m % 2], pg[:, m % 2], pp[:, m], ALU.mult)
                    dve.drain()
                    dve.tensor_tensor(x_res[:, m], x_res[:, m], pg[:, m % 2], ALU.add).then_inc(pg_chan.free, 1)
                    dve.drain().then_inc(x_new, 1)


def _rows(a, per):
    k, n = a.shape
    return a.reshape(k // (P * per), per, P, n).transpose(0, 2, 1, 3).reshape(-1, P, per * n)


def _cols(a):
    k, n = a.shape
    return a.reshape(k // P, P, n // P, P).transpose(2, 1, 0, 3).reshape(-1, P, k)


def _units(L, w_in, w_branch, w_out, peer_wq, peer_u, peer_v, w_ple_gate, w_ple_proj):
    at, part = 0, {}
    conv = D_INNER + 2 * GROUPS * D_STATE
    for n, wd in (("z", D_INNER), ("xbc", conv), ("dt", SSM_HEADS), ("q", ATT_HEADS * ATT_D), ("k", KV_HEADS * ATT_D),
                  ("v", KV_HEADS * ATT_D), ("qi", IDX_HEADS * IDX_D), ("ki", IDX_D), ("wi", IDX_HEADS),
                  ("g_ssm", D_MODEL), ("g_att", D_MODEL)):
        part[n] = w_in[L][:, at:at + wd]
        at += wd
    fill = np.zeros((D_MODEL, P - IDX_D - IDX_HEADS - SSM_HEADS), np.float32)
    out = [_rows(part["qi"], 2), _rows(np.concatenate([part["ki"], part["wi"], part["dt"], fill], 1), KT)]

    def branch(rows):
        return (rows.reshape(4, P, 4, 2, P).transpose(2, 1, 3, 0, 4).reshape(4, P, UNIT))

    gates = np.stack([_cols(part["g_att"]), _cols(part["g_ssm"])], 1).reshape(-1, P, UNIT)
    at = sum(GATE_AT[:2])
    out.append(gates[:at])
    qw = REP * ATT_D
    for g in range(KV_HEADS):
        d = slice(g * ATT_D, (g + 1) * ATT_D)
        out += [_rows(part["q"][:, g * qw:(g + 1) * qw], 2),
                _rows(np.concatenate([part["k"][:, d], part["v"][:, d]], 1), 4), gates[at:at + GATE_AT[2 + g]],
                branch(w_branch[L][D_INNER + g * qw:D_INNER + (g + 1) * qw])]
        at += GATE_AT[2 + g]
    for g in range(GROUPS):
        b0 = D_INNER + g * D_STATE
        c0 = b0 + GROUPS * D_STATE
        s = slice(g * GW, (g + 1) * GW)
        out += [_cols(part["xbc"][:, b0:b0 + D_STATE]), _cols(part["xbc"][:, c0:c0 + D_STATE]),
                _cols(part["xbc"][:, s]), _rows(part["z"][:, s], 2), branch(w_branch[L][s])]
        if g > 0:
            out[-6], out[-5] = out[-5], out[-6]
    out += [_cols(w_out[L]), _cols(peer_wq[L])]
    u = peer_u[L].reshape(N_KEYS, N_KEYS, KT, P).transpose(1, 3, 2, 0).reshape(BLOCKS, NB, P, UNIT)
    v = peer_v[L].reshape(N_KEYS, N_KEYS, D_MODEL).transpose(1, 0, 2).reshape(BLOCKS, NB, P, UNIT)
    e = BLOCKS // 2
    out += [u[:e + 1].reshape(-1, P, UNIT), v[:e + 1].reshape(-1, P, UNIT),
            np.concatenate([u[e + 1:], v[e + 1:]], 1).reshape(-1, P, UNIT)]
    pj = w_ple_proj[L].reshape(2, P, 2, 4, P).transpose(2, 1, 3, 0, 4).reshape(2, P, UNIT)
    out += [pj, _cols(w_ple_gate[L]), np.zeros((U_PAD, P, UNIT), np.float32)]
    return np.concatenate(out, 0)


def _params(L, a):
    order = []
    for g in range(GROUPS):
        order += [D_INNER // P + g, D_INNER // P + GROUPS + g] + [g * GW // P + i for i in range(GW // P)]
    rows = lambda v: np.broadcast_to(v[None], (P, v.shape[0]))
    cw = a["conv_w"][L].reshape(-1, P, CONV_W)[order].transpose(1, 0, 2).reshape(P, -1)
    cb = a["conv_b"][L].reshape(-1, P)[order].T
    return np.concatenate([a["norm_mix"][L].reshape(KT, P).T, a["norm_ffn"][L].reshape(KT, P).T,
                           a["norm_ple"][L].reshape(KT, P).T, cw, cb, a["ssm_norm"][L].reshape(-1, P).T,
                           rows(a["dt_bias"][L]), rows(a["a_log"][L]), rows(a["d_skip"][L]),
                           rows(a["q_norm"][L]), rows(a["k_norm"][L])], 1)


def _constants():
    i = np.arange(P)
    f = np.float32
    inv = [f(1) / (f(10000.0) ** (np.arange(0, d, 2, dtype=f) / f(d))) for d in (ATT_D, IDX_D)]
    row = lambda v: np.broadcast_to(np.asarray(v, f)[None], (P, len(v)))
    return np.concatenate([np.eye(P, dtype=f), np.ones((P, P), f), (i[None] >= i[:, None]).astype(f),
                           np.where(i[None] > i[:, None], f(BIG), f(0)), row(i), row(inv[0]), row(inv[1])], 1)


def kernel(**inputs):
    import concourse.bacc as bacc
    from concourse.bass_utils import run_bass_kernel_spmd

    a = {n: np.asarray(v) for n, v in inputs.items()}
    arrays = {
        "w": np.concatenate([_units(L, *(a[n] for n in ("w_in", "w_branch", "w_out", "peer_wq", "peer_u", "peer_v",
                                                        "w_ple_gate", "w_ple_proj"))) for L in range(DEPTH)], 0),
        "par": np.ascontiguousarray(np.stack([_params(L, a) for L in range(DEPTH)], 1)),
        "cst": np.ascontiguousarray(_constants()),
        "pos": np.ascontiguousarray(a["positions"].reshape(NT, P).T.astype(np.int32)),
        "x": np.ascontiguousarray(a["x"].reshape(SEQ, KT, P).transpose(2, 1, 0)),
        "p_emb": np.ascontiguousarray(a["p"].reshape(DEPTH, SEQ, PLE // P, P).transpose(0, 3, 2, 1)),
        "keys": np.ascontiguousarray(a["peer_keys"].reshape(DEPTH, 2 * PEER_HEADS, N_KEYS, P).transpose(0, 3, 1, 2)),
    }
    nc = bacc.Bacc("TRN2", target_bir_lowering=False, num_devices=1)
    aps = {n: nc.dram_tensor("in_" + n, v.shape, mybir.dt.from_np(v.dtype), kind="ExternalInput").ap()
           for n, v in arrays.items()}
    gates = nc.dram_tensor("gates", (DEPTH, N_GRP, P, N_KEYS, GRP), F32, kind="Internal").ap()
    early = nc.dram_tensor("early_gelu", (DEPTH, EARLY, P, SEQ), F32, kind="Internal").ap()
    mix_gates = nc.dram_tensor("mix_gates", (DEPTH, 2 * KT, P, SEQ), F32, kind="Internal").ap()
    out = nc.dram_tensor("out_x", (P, KT, SEQ), F32, kind="ExternalOutput").ap()
    build(nc, aps["w"], aps["par"], aps["cst"], aps["pos"], aps["x"], aps["p_emb"], aps["keys"], gates, early,
          mix_gates, out, DEPTH)
    r = run_bass_kernel_spmd(nc, [{"in_" + n: v for n, v in arrays.items()}], core_ids=[0])
    return r.results[0]["out_x"].transpose(2, 1, 0).reshape(1, SEQ, D_MODEL)
```
